# Optimizing a Trainium2 kernel written in Bass

```python
import jax, jax.numpy as jnp
from jax import lax
import numpy as np

D_MODEL = 1024
BATCH = 1
SEQ = 512
DEPTH = 2

N_MIXERS = 2
N_SSD_LAYERS = (DEPTH + 1) // 2
N_DSA_LAYERS = DEPTH // 2
EPS = 1e-6

SSD_EXPAND = 2
SSD_D_INNER = SSD_EXPAND * D_MODEL
SSD_HEAD_DIM = 64
SSD_HEADS = SSD_D_INNER // SSD_HEAD_DIM
SSD_GROUPS = 8
SSD_HEADS_PER_GROUP = SSD_HEADS // SSD_GROUPS
SSD_STATE = 128
SSD_CONV = 4
SSD_CHUNK = 128
SSD_GN = SSD_GROUPS * SSD_STATE
SSD_CONV_DIM = SSD_D_INNER + 2 * SSD_GN
SSD_PROJ = SSD_D_INNER + SSD_CONV_DIM + SSD_HEADS

ATT_HEADS = 16
ATT_KV_HEADS = 4
ATT_Q_PER_KV = ATT_HEADS // ATT_KV_HEADS
ATT_HEAD_DIM = 64
IDX_HEADS = 8
IDX_HEAD_DIM = 64
TOPK_MAX = 256
Q_BLOCK = 128
DSA_Q_END = ATT_HEADS * ATT_HEAD_DIM
DSA_K_END = DSA_Q_END + ATT_KV_HEADS * ATT_HEAD_DIM
DSA_V_END = DSA_K_END + ATT_KV_HEADS * ATT_HEAD_DIM
DSA_QI_END = DSA_V_END + IDX_HEADS * IDX_HEAD_DIM
DSA_KI_END = DSA_QI_END + IDX_HEAD_DIM
DSA_PROJ = DSA_KI_END + IDX_HEADS

MOE_GROUPS = 4
MOE_EXPERTS_PER_GROUP = 4
MOE_EXPERTS = MOE_GROUPS * MOE_EXPERTS_PER_GROUP
MOE_TOPK = 2
MOE_HIDDEN = 256

kernel_name = "hybrid_ssd_dsa_hmoe_adaln"

def rms_norm(x):
    xf = x.astype(jnp.float32)
    return (xf * lax.rsqrt(jnp.mean(xf * xf, axis=-1, keepdims=True) + EPS)).astype(x.dtype)

def causal_depthwise_conv(u, w, b):
    k = w.shape[0]
    out = lax.conv_general_dilated(
        u, w[:, None, :].astype(u.dtype), window_strides=(1,), padding=[(k - 1, 0)],
        dimension_numbers=('NWC', 'WIO', 'NWC'), feature_group_count=u.shape[-1])
    return out + b

def ssd_chunked_scan(X, A, Bm, Cm):
    b, l, g, j, p = X.shape
    n = Bm.shape[-1]
    q = SSD_CHUNK
    c = l // q
    Xc = X.reshape(b, c, q, g, j, p)
    Bc = Bm.reshape(b, c, q, g, n)
    Cc = Cm.reshape(b, c, q, g, n)
    A = A.reshape(b, c, q, g, j).transpose(0, 1, 3, 4, 2)
    A_cs = jnp.cumsum(A, axis=-1)
    tril = jnp.tril(jnp.ones((q, q), dtype=bool))
    seg = A_cs[..., :, None] - A_cs[..., None, :]
    decay_in = jnp.exp(jnp.where(tril, seg, -jnp.inf))
    cb = jnp.einsum('bclgn,bcsgn->bcgls', Cc, Bc)
    y_diag = jnp.einsum('bcgjls,bcsgjp->bclgjp', cb[:, :, :, None] * decay_in, Xc)
    decay_to_end = jnp.exp(A_cs[..., -1:] - A_cs).transpose(0, 1, 4, 2, 3)
    states = jnp.einsum('bcsgn,bcsgjp->bcgjpn', Bc, Xc * decay_to_end[..., None])
    chunk_decay = jnp.exp(A_cs[..., -1])

    def step(carry, inp):
        st, dec = inp
        return carry * dec[..., None, None] + st, carry

    init = jnp.zeros((b, g, j, p, n), states.dtype)
    _, prev = lax.scan(step, init, (jnp.moveaxis(states, 1, 0), jnp.moveaxis(chunk_decay, 1, 0)))
    prev = jnp.moveaxis(prev, 0, 1)
    decay_from_start = jnp.exp(A_cs).transpose(0, 1, 4, 2, 3)
    y_off = jnp.einsum('bclgn,bcgjpn->bclgjp', Cc, prev) * decay_from_start[..., None]
    return (y_diag + y_off).reshape(b, l, g, j, p)

def ssd_mixer(h, w_in, conv_w, conv_b, dt_bias, a_log, d_skip, norm_w, w_out):
    b, l, _ = h.shape
    G, J, P = SSD_GROUPS, SSD_HEADS_PER_GROUP, SSD_HEAD_DIM
    proj = h @ w_in
    z = proj[..., :SSD_D_INNER]
    xbc = proj[..., SSD_D_INNER:SSD_D_INNER + SSD_CONV_DIM]
    dt = proj[..., SSD_D_INNER + SSD_CONV_DIM:]
    xbc = jax.nn.silu(causal_depthwise_conv(xbc, conv_w, conv_b))
    xs = xbc[..., :SSD_D_INNER].reshape(b, l, G, J, P)
    Bm = xbc[..., SSD_D_INNER:SSD_D_INNER + SSD_GN].reshape(b, l, G, SSD_STATE)
    Cm = xbc[..., SSD_D_INNER + SSD_GN:].reshape(b, l, G, SSD_STATE)
    dt = jax.nn.softplus((dt + dt_bias).astype(jnp.float32)).reshape(b, l, G, J)
    A = -jnp.exp(a_log.astype(jnp.float32)).reshape(G, J)
    y = ssd_chunked_scan(xs * dt[..., None], dt * A, Bm, Cm)
    y = y + xs * d_skip.reshape(G, J, 1)
    y = y * jax.nn.silu(z).reshape(b, l, G, J, P)
    y = rms_norm(y.reshape(b, l, G, J * P)) * norm_w.reshape(G, J * P)
    return y.reshape(b, l, SSD_D_INNER).astype(h.dtype) @ w_out

def dsa_mixer(h, w_in, q_norm, k_norm, w_out):
    b, l, _ = h.shape
    proj = h @ w_in
    q = proj[..., :DSA_Q_END].reshape(b, l, ATT_KV_HEADS, ATT_Q_PER_KV, ATT_HEAD_DIM)
    k = proj[..., DSA_Q_END:DSA_K_END].reshape(b, l, ATT_KV_HEADS, ATT_HEAD_DIM)
    v = proj[..., DSA_K_END:DSA_V_END].reshape(b, l, ATT_KV_HEADS, ATT_HEAD_DIM)
    qi = proj[..., DSA_V_END:DSA_QI_END].reshape(b, l, IDX_HEADS, IDX_HEAD_DIM)
    ki = proj[..., DSA_QI_END:DSA_KI_END]
    wi = proj[..., DSA_KI_END:]
    q = rms_norm(q) * q_norm
    k = rms_norm(k) * k_norm
    topk = min(TOPK_MAX, l // 4)
    nb = l // Q_BLOCK

    def to_blocks(t):
        return jnp.moveaxis(t.reshape((b, nb, Q_BLOCK) + t.shape[2:]), 1, 0)

    starts = jnp.arange(nb, dtype=jnp.int32) * Q_BLOCK
    key_pos = jnp.arange(l, dtype=jnp.int32)
    gather = jax.vmap(lambda table, idx: table[idx])

    def attend_block(args):
        q_b, qi_b, wi_b, start = args
        q_pos = start + jnp.arange(Q_BLOCK, dtype=jnp.int32)
        rel = jax.nn.relu(jnp.einsum('bthe,bse->bhts', qi_b, ki).astype(jnp.float32) * IDX_HEAD_DIM ** -0.5)
        score = jnp.einsum('bth,bhts->bts', wi_b.astype(jnp.float32) * IDX_HEADS ** -0.5, rel)
        causal = key_pos[None, :] <= q_pos[:, None]
        score = jnp.where(causal[None], score, -jnp.inf)
        _, idx = lax.top_k(score, topk)
        valid = idx <= q_pos[None, :, None]
        k_sel = gather(k, idx)
        v_sel = gather(v, idx)
        s = jnp.einsum('bthgd,btkhd->bthgk', q_b, k_sel).astype(jnp.float32) * ATT_HEAD_DIM ** -0.5
        s = jnp.where(valid[:, :, None, None, :], s, -jnp.inf)
        p = jax.nn.softmax(s, axis=-1)
        return jnp.einsum('bthgk,btkhd->bthgd', p.astype(v.dtype), v_sel)

    o = lax.map(attend_block, (to_blocks(q), to_blocks(qi), to_blocks(wi), starts))
    o = jnp.moveaxis(o, 0, 1).reshape(b, l, ATT_HEADS * ATT_HEAD_DIM)
    return o @ w_out

def hierarchical_moe(h, w_group, b_group, w_expert, b_expert, w1, w3, w2):
    b, l, d = h.shape
    t = h.reshape(-1, d)
    g_prob = jax.nn.softmax((t @ w_group + b_group).astype(jnp.float32), axis=-1)
    g_val, g_idx = lax.top_k(g_prob, 1)
    e_logits = (t @ w_expert + b_expert).astype(jnp.float32).reshape(-1, MOE_GROUPS, MOE_EXPERTS_PER_GROUP)
    in_group = jnp.take_along_axis(e_logits, g_idx[:, :, None], axis=1)[:, 0]
    e_val, e_idx = lax.top_k(in_group, MOE_TOPK)
    e_w = jax.nn.softmax(e_val, axis=-1) * g_val
    expert_id = g_idx * MOE_EXPERTS_PER_GROUP + e_idx
    combine = jnp.sum(jax.nn.one_hot(expert_id, MOE_EXPERTS, dtype=jnp.float32) * e_w[..., None], axis=1)
    hid = jax.nn.silu(jnp.einsum('td,edf->tef', t, w1)) * jnp.einsum('td,edf->tef', t, w3)
    out = jnp.einsum('tef,efd->td', hid * combine[..., None].astype(hid.dtype), w2)
    return out.reshape(b, l, d)

def setup_inputs(seed: int = 0) -> dict:
    key = jax.random.key(seed)
    ks = jax.random.split(key, 25)

    def nrm(k, shape, scale):
        return jax.random.normal(k, shape, jnp.float32) * scale

    D = D_MODEL
    dt0 = jnp.exp(jax.random.uniform(ks[9], (N_SSD_LAYERS, SSD_HEADS), jnp.float32,
                                     minval=float(np.log(1e-3)), maxval=float(np.log(1e-1))))
    return {
        "x": nrm(ks[0], (BATCH, SEQ, D), 1.0),
        "c": nrm(ks[1], (BATCH, D), 1.0),
        "ada_w": nrm(ks[2], (DEPTH, D, 6 * D), D ** -0.5),
        "ada_b": nrm(ks[3], (DEPTH, 6 * D), 0.01),
        "norm_mix": 1.0 + nrm(ks[4], (DEPTH, D), 0.02),
        "norm_ffn": 1.0 + nrm(ks[5], (DEPTH, D), 0.02),
        "ssd_w_in": nrm(ks[6], (N_SSD_LAYERS, D, SSD_PROJ), D ** -0.5),
        "ssd_conv_w": nrm(ks[7], (N_SSD_LAYERS, SSD_CONV, SSD_CONV_DIM), SSD_CONV ** -0.5),
        "ssd_conv_b": nrm(ks[8], (N_SSD_LAYERS, SSD_CONV_DIM), 0.01),
        "ssd_dt_bias": dt0 + jnp.log(-jnp.expm1(-dt0)),
        "ssd_a_log": jnp.log(jax.random.uniform(ks[10], (N_SSD_LAYERS, SSD_HEADS), jnp.float32, minval=1.0, maxval=16.0)),
        "ssd_d": 1.0 + nrm(ks[11], (N_SSD_LAYERS, SSD_HEADS), 0.02),
        "ssd_norm": 1.0 + nrm(ks[12], (N_SSD_LAYERS, SSD_D_INNER), 0.02),
        "ssd_w_out": nrm(ks[13], (N_SSD_LAYERS, SSD_D_INNER, D), SSD_D_INNER ** -0.5),
        "dsa_w_in": nrm(ks[14], (N_DSA_LAYERS, D, DSA_PROJ), D ** -0.5),
        "dsa_q_norm": 1.0 + nrm(ks[15], (N_DSA_LAYERS, ATT_HEAD_DIM), 0.02),
        "dsa_k_norm": 1.0 + nrm(ks[16], (N_DSA_LAYERS, ATT_HEAD_DIM), 0.02),
        "dsa_w_out": nrm(ks[17], (N_DSA_LAYERS, ATT_HEADS * ATT_HEAD_DIM, D), (ATT_HEADS * ATT_HEAD_DIM) ** -0.5),
        "moe_w_group": nrm(ks[18], (DEPTH, D, MOE_GROUPS), D ** -0.5),
        "moe_b_group": nrm(ks[19], (DEPTH, MOE_GROUPS), 0.01),
        "moe_w_expert": nrm(ks[20], (DEPTH, D, MOE_EXPERTS), D ** -0.5),
        "moe_b_expert": nrm(ks[21], (DEPTH, MOE_EXPERTS), 0.01),
        "moe_w1": nrm(ks[22], (DEPTH, MOE_EXPERTS, D, MOE_HIDDEN), D ** -0.5),
        "moe_w3": nrm(ks[23], (DEPTH, MOE_EXPERTS, D, MOE_HIDDEN), D ** -0.5),
        "moe_w2": nrm(ks[24], (DEPTH, MOE_EXPERTS, MOE_HIDDEN, D), MOE_HIDDEN ** -0.5),
    }

def reference(x, c, ada_w, ada_b, norm_mix, norm_ffn, ssd_w_in, ssd_conv_w, ssd_conv_b, ssd_dt_bias,
              ssd_a_log, ssd_d, ssd_norm, ssd_w_out, dsa_w_in, dsa_q_norm, dsa_k_norm, dsa_w_out,
              moe_w_group, moe_b_group, moe_w_expert, moe_b_expert, moe_w1, moe_w3, moe_w2):
    cond = jax.nn.silu(c)
    for i in range(DEPTH):
        mod = (cond @ ada_w[i] + ada_b[i])[:, None, :]
        shift_m, scale_m, gate_m, shift_f, scale_f, gate_f = jnp.split(mod, 6, axis=-1)
        h = rms_norm(x) * norm_mix[i] * (1.0 + scale_m) + shift_m
        j = i // N_MIXERS
        if i % N_MIXERS == 0:
            y = ssd_mixer(h, ssd_w_in[j], ssd_conv_w[j], ssd_conv_b[j], ssd_dt_bias[j], ssd_a_log[j],
                          ssd_d[j], ssd_norm[j], ssd_w_out[j])
        else:
            y = dsa_mixer(h, dsa_w_in[j], dsa_q_norm[j], dsa_k_norm[j], dsa_w_out[j])
        x = x + gate_m * y
        h = rms_norm(x) * norm_ffn[i] * (1.0 + scale_f) + shift_f
        x = x + gate_f * hierarchical_moe(h, moe_w_group[i], moe_b_group[i], moe_w_expert[i], moe_b_expert[i],
                                          moe_w1[i], moe_w3[i], moe_w2[i])
    return x


_drawn_inputs = setup_inputs


def setup_inputs(seed=0):
    import zlib

    import numpy as np

    out = dict(_drawn_inputs(seed))
    spreads = {}
    factors = {'dsa_q_norm': 8.0, 'dsa_k_norm': 5.515, 'moe_b_group': 2.696, 'moe_b_expert': 4.216}
    for name, (base, spread) in spreads.items():
        noise = np.random.default_rng([zlib.crc32(name.encode()), seed]).standard_normal(out[name].shape)
        drawn = base * np.exp(spread * noise) if base else spread * noise
        out[name] = __import__('jax').numpy.asarray(drawn.astype(out[name].dtype))
    for name, factor in factors.items():
        out[name] = (out[name] * factor).astype(out[name].dtype)
    return out
```

```python
from contextlib import ExitStack

import numpy as np

import concourse.bass as bass
from concourse import mybir

F32 = mybir.dt.float32
I32 = mybir.dt.int32
ALU = mybir.AluOpType
ACT = mybir.ActivationFunctionType
AX = mybir.AxisListType

P = 128
D = 1024
SEQ = 512
NT = SEQ // P
KD = D // P
EPS = 1e-6
NEG = -1e30
TAKEN = -3e38

DI = 2048
G = 8
HEADS = 32
HD = 64
NS = 128
GC = DI // G
JH = HEADS // G
OFF_Z, OFF_X, OFF_B, OFF_C, OFF_DT = 0, DI, 2 * DI, 2 * DI + G * NS, 2 * DI + 2 * G * NS
CT = DI // P
CONV_TILES = (DI + 2 * G * NS) // P
GW = 2 * GC + 2 * NS
LOG1P_TERMS = 8

QH, KVH = 16, 4
IH = 8
TOPK = min(256, SEQ // 4)
QK_HEADS = QH + KVH
OFF_Q, OFF_K, OFF_V = 0, 1024, 1280
OFF_QI, OFF_KI, OFF_WI = 1536, 2048, 2112

NG, EG = 4, 4
NE = NG * EG
FH = 256
OVER = 2 * SEQ // (P + 1)
NB = NE + OVER

ADA_SLOT = KD * D
EXPERT_SLOT = KD * 2 * FH + 2 * D


PER_USE = {
    "n_sq": NT, "n_rs": 1, "n_xn": NT, "n_col": 1, "n_tr": KD, "n_ev0": KD // 2, "n_ev1": KD // 2,
    "p_gate": KD, "pe_gate": KD, "d_gate": 2, "x_up": NT,
    "xn_stored": 16, "rt_in": 64, "pe_rt": 1, "d_g": 1, "d_e": 1, "a_r": 2, "d_m": 1, "pe_rank": 1, "d_r": 1,
    "pe_idx": 1, "d_idx": 1, "over_ids": 1,
    "exp13_0": 32 * ((NB + 1) // 2), "exp13_1": 32 * (NB // 2), "exp2_0": 16 * ((NB + 1) // 2), "exp2_1": 16 * (NB // 2),
    "gath_0": 16 * ((NB + 1) // 2), "gath_1": 16 * (NB // 2), "y_stored_0": 16 * ((NB + 1) // 2), "y_stored_1": 16 * (NB // 2),
    "pe_t": 2 * NB, "t_ev0": NB, "t_ev1": NB, "pe_h": NB, "a_mt": NB, "d_hid": NB, "pe_ht": NB, "a_ht": NB, "pe_o": NB,
    "a_yo": NB, "d_yo": NB, "yg_0": 32 * (NT // 2), "yg_1": 32 * (NT // 2),
}
CREDIT = ("pe_df", "pe_st", "pe_yt", "d_bt", "a_yn", "a_ye", "d_skip", "d_cb", "d_w", "d_y", "d_st", "d_mu",
          "d_ad", "p_y")


def build(nc, t):
    with ExitStack() as ctx:
        def sb(name, shape, dt=F32):
            return ctx.enter_context(nc.sbuf_tensor(name, shape, dt))

        sems = {}

        def sem(name):
            name = name.split(".")[0]
            if name not in sems:
                sems[name] = ctx.enter_context(nc.semaphore(name))
            return sems[name]

        def count(name, value):
            base, _, use = name.partition(".")
            if use:
                value = value + (int(use) - (base == "x_up")) * PER_USE[base]
            return value + (base in CREDIT)

        def due(value):
            return not isinstance(value, int) or value > 0

        def chunks_before(u):
            tt, kv = max(u, 0) // 4, max(u, 0) % 4
            return 4 * (tt * (tt + 1) // 2) + kv * (tt + 1)

        def credit(eng, names):
            for name in names:
                eng.sem_inc(sem(name), 1)

        bank = [ctx.enter_context(nc.psum_tensor(f"bank{i}", [P, 512], F32)) for i in range(8)]
        xn_dram = [nc.dram_tensor(f"xn_rows{l}", (SEQ, D), F32, kind="Internal").ap() for l in range(2)]
        y_dram = [nc.dram_tensor(f"slot_rows{l}", (NB * P, D), F32, kind="Internal").ap() for l in range(2)]

        x = sb("x_res", [P, NT, D])
        xn = sb("xn", [P, NT, D])
        hT = sb("hT", [P, KD, SEQ])
        wts = sb("wts", [P, 2 * EXPERT_SLOT + ADA_SLOT])
        ident = sb("ident", [P, P])
        upto = sb("upto", [P, P])
        after = sb("after", [P, P])
        before = sb("before", [P, P])
        causal = sb("causal", [P, P])
        ones = sb("ones", [P, P])
        iota = sb("iota", [P, P])
        tokid = sb("tokid", [P, NT])
        pref = sb("pref", [P, NT, 4])
        ccol = sb("ccol", [P, KD])
        cond = sb("cond", [P, KD])
        modcol = sb("modcol", [P, 12, KD])
        adab = sb("adab", [P, 12, KD])
        normw = sb("normw", [P, 4, KD])
        acol = sb("acol", [P, 4, KD])
        ssq = sb("ssq", [P, 4, NT])
        rstd = sb("rstd", [P, 4, NT])
        expo = sb("expo", [P, QK_HEADS])

        epst = sb("epst", [P, 1])
        work = sb("work", [P, 18944])

        class Carve:
            def __init__(self):
                self.at = 0

            def __call__(self, *shape, dt=F32):
                n = int(np.prod(shape))
                v = work[:, self.at:self.at + n]
                self.at += n
                assert self.at <= 18944, self.at
                if dt is not F32:
                    v = v.bitcast(dt)
                if len(shape) == 2:
                    v = v.rearrange("p (a b) -> p a b", b=shape[1])
                if len(shape) == 3:
                    v = v.rearrange("p (a b c) -> p a b c", b=shape[1], c=shape[2])
                return v

        xn_flat = xn[:].rearrange("p t d -> p (t d)")
        slot = [wts[:, i * EXPERT_SLOT:(i + 1) * EXPERT_SLOT] for i in range(2)]
        ada_buf = wts[:, 2 * EXPERT_SLOT:]

        cv = Carve()
        yT = cv(CT, SEQ)
        zs = [cv(NT, GC) for _ in range(2)]
        upad = [cv(516) for _ in range(2)]
        cacc = [cv(SEQ) for _ in range(2)]
        th = [cv(SEQ) for _ in range(2)]
        xdt, skip, xd, yb, yn, zt, state = (cv(GC) for _ in range(7))
        decay, wmat = cv(JH, P), cv(JH, P)
        btok, cbm = cv(P), cv(P)
        tria = [cv(JH, P) for _ in range(2)]
        dtw = xd.rearrange("p (k h) -> p k h", h=HEADS)
        s1, s2 = (v.rearrange("p (t h) -> p t h", h=HEADS) for v in (btok, cbm))
        dt, aa, acs, ea, dte, s3 = (cv(NT, HEADS) for _ in range(6))
        dtb, alog, dsk = cv(HEADS), cv(HEADS), cv(HEADS)
        prow, brow = th[0][:, 0:P], th[1][:, 0:P]
        cwT = cv(5, CONV_TILES)
        nwT = cv(CT)
        gp = [cv(4, 5) for _ in range(2)]
        gn_w = [cv(2) for _ in range(2)]
        yss, yrs = cv(1), cv(1)
        gatebc0 = zs[0].rearrange("p a b -> p (a b)")
        diag0 = tria[0][:, 0, :]
        xbcT = [xn_flat[:, i * 2048:(i + 1) * 2048].rearrange("p (a b) -> p a b", b=SEQ) for i in range(2)]

        mv = Carve()
        xg = [mv(D) for _ in range(2)]
        xgT = [mv(KD, P) for _ in range(2)]
        mth, mh1, hid = mv(FH), mv(FH), mv(FH)
        hidT = mv(2, P)
        yo = [mv(D) for _ in range(2)]
        yg = [[mv(D) for _ in range(2)] for _ in range(2)]
        gatebc = mv(D)
        rtw = mv(KD, NG + NE)
        rtb = mv(NG + NE)
        lg = mv(NT, NG + NE)
        gsh, cand, goh, ein, oh1, oh2, m4 = (mv(NT, 4) for _ in range(7))
        prod = mv(NT, NE)
        M1, M2, MM, rank, toff = (mv(NT, NE) for _ in range(5))
        g1, g2, g3, wc1, wc2, mx1, mx2 = (mv(NT) for _ in range(7))
        tot, over, cumi, base2 = (mv(NE) for _ in range(4))
        rr, kk, rmod, blk, slf = (mv(2, NT) for _ in range(5))
        sloti = mv(2, NT, dt=I32)
        R = [mv(P) for _ in range(8)]
        Bm = mv(8, NB)
        idx = mv(NB, dt=I32)
        ovt = mv(OVER, NE)
        ovf = mv(OVER)
        ovi = mv(OVER, dt=I32)
        mdiag = mv(P)

        av = Carve()
        qkn = av(QH * HD + 2 * KVH * HD)
        V = av(NT, KVH * HD)
        qT = av(8, SEQ)
        kT = av(KVH, SEQ)
        qiT = av(4, SEQ)
        kiT = av(SEQ)
        sel = av(NT, SEQ)
        PT = av(4, 4 * P)
        o = av(D)
        oT = av(KD, P)
        kiw = o.rearrange("p (k n) -> p k n", k=KD)
        rel = [oT[:, 4 * i:4 * i + 4, :].rearrange("p a b -> p (a b)") for i in range(2)]
        wiw = av(KD, IH)
        wi = av(NT, IH)
        hss, hrs = av(QK_HEADS), av(QK_HEADS)
        qkw = av(2)
        max8 = av(8)
        nmx, rsum, rinv = av(4, 4), av(QH), av(QH)
        gatebc1 = av(D)
        adiag = av(P)
        Sm = [xn_flat[:, i * 2048:(i + 1) * 2048].rearrange("p (a b) -> p a b", b=SEQ) for i in range(2)]
        sqs = xn_flat[:, 0:QK_HEADS * HD]

        w13 = [s[:, 0:KD * 2 * FH].rearrange("p (k f) -> p k f", k=KD) for s in slot]
        w2s = [s[:, KD * 2 * FH:].rearrange("p (k n) -> p k n", k=2) for s in slot]
        gw = [s.rearrange("p (k f) -> p k f", k=KD) for s in slot]
        wo_ssd = [wts[:, i * 4096:(i + 1) * 4096].rearrange("p (c n) -> p c n", c=4) for i in range(3)]
        ada = [ada_buf.rearrange("p (k n) -> p k n", k=KD), wts[:, 0:ADA_SLOT].rearrange("p (k n) -> p k n", k=KD)]
        wq = [ada_buf[:, i * 4096:(i + 1) * 4096].rearrange("p (k f) -> p k f", k=KD) for i in range(2)]
        wkv = wts[:, 0:4096].rearrange("p (k f) -> p k f", k=KD)
        wqi = wts[:, 4096:8192].rearrange("p (k f) -> p k f", k=KD)
        wo_dsa = ada_buf.rearrange("p (c n) -> p c n", c=KD)

        w_in = t["ssd_w_in"][0].rearrange("(p k) n -> p k n", k=KD)
        ada_d = t["ada_w"].rearrange("l (p k) (j n) -> l j p k n", k=KD, j=6)
        dsa_in = t["dsa_w_in"][0].rearrange("(p k) n -> p k n", k=KD)

        def bc(ap, n):
            return ap.unsqueeze(2).broadcast_to([ap.shape[0], ap.shape[1], n])

        def rep(ap, n):
            return ap.unsqueeze(1).broadcast_to([ap.shape[0], n, ap.shape[1]])

        def row_bc(ap, n):
            return ap.rearrange("(o n) -> o n", o=1).broadcast_to([P, n])

        block = ctx.enter_context(nc.Block())

        @block.sync
        def _(sp):
            def load_ada(i, buf, s):
                sp.dma_start(buf, ada_d[i // 6, i % 6]).then_inc(s, 16)

            def load_group(g, par):
                s = sem(f"group_w{par}")
                for dst, col, n in ((0, OFF_X, GC), (GC, OFF_B, NS), (GC + NS, OFF_C, NS), (GC + 2 * NS, OFF_Z, GC)):
                    sp.dma_start(gw[par][:, :, dst:dst + n], w_in[:, :, bass.DynSlice(g * n + col, n)]).then_inc(s, 16)

            sp.dma_start(ccol[:], t["c"][0].rearrange("(p k) -> p k", k=KD)).then_inc(sem("c_in"), 16)
            load_ada(0, ada[0], sem("ada_in0"))
            sp.dma_start(x[:], t["x"][0].rearrange("(t p) d -> p t d", p=P)).then_inc(sem("x_in"), 16)
            load_ada(1, ada[1], sem("ada_in1"))
            s = sem("par_in")
            sp.dma_start(adab[:], t["ada_b"].rearrange("l (j p k) -> p (l j) k", j=6, k=KD)).then_inc(s, 16)
            sp.dma_start(normw[:, 0:4:2], t["norm_mix"].rearrange("l (p k) -> p l k", k=KD)).then_inc(s, 16)
            sp.dma_start(normw[:, 1:4:2], t["norm_ffn"].rearrange("l (p k) -> p l k", k=KD)).then_inc(s, 16)
            sp.dma_start(dtw, w_in[:, :, OFF_DT:OFF_DT + HEADS]).then_inc(s, 16)
            sp.dma_start(dtb, row_bc(t["ssd_dt_bias"][0], HEADS)).then_inc(s, 16)
            sp.dma_start(alog, row_bc(t["ssd_a_log"][0], HEADS)).then_inc(s, 16)
            sp.dma_start(dsk, row_bc(t["ssd_d"][0], HEADS)).then_inc(s, 16)
            sp.dma_start(prow, t["ssd_conv_w"][0].rearrange("a (c p) -> (a c) p", p=P)).then_inc(s, 16)
            sp.dma_start(brow[0:CONV_TILES, :], t["ssd_conv_b"][0].rearrange("(c p) -> c p", p=P)).then_inc(s, 16)
            sp.dma_start(brow[CONV_TILES:CONV_TILES + CT, :], t["ssd_norm"][0].rearrange("(c p) -> c p", p=P)).then_inc(s, 16)
            sp.wait_ge(sem("pe_ada"), 1)
            load_ada(2, ada[0], sem("ada_in0"))
            sp.wait_ge(sem("pe_ada"), 2)
            load_group(0, 0)
            load_group(1, 1)

            def ssd_loads(g, par, last):
                if not last:
                    sp.wait_ge(sem("pe_z"), g * NT + NT)
                    load_group(g + 2, par)
                sp.wait_ge(sem("pe_ad"), g * NT + NT)
                load_ada(g + 3, ada[0], sem("ada_in0"))
            for g in range(G):
                ssd_loads(g, g % 2, g >= G - 2)
            for c in range(3):
                if c == 0:
                    sp.wait_ge(sem("pe_z"), NT * G)
                sp.dma_start(wo_ssd[c], t["ssd_w_out"][0, c * 512:(c + 1) * 512, :].rearrange("(c p) n -> p c n", p=P)
                             ).then_inc(sem(f"wo_in{c}"), 16)
            sp.wait_ge(sem("pe_wo"), 1)
            sp.dma_start(wo_ssd[0], t["ssd_w_out"][0, 1536:2048, :].rearrange("(c p) n -> p c n", p=P)
                         ).then_inc(sem("wo_in0"), 16)
            sp.wait_ge(sem("pe_ada"), 3)
            load_ada(11, ada[0], sem("ada_in0"))

            def load_expert(l, e, par):
                s = sem(f"exp13_{par}.{l}")
                for i, w in enumerate(("moe_w1", "moe_w3")):
                    src = t[w][l].rearrange("e (p k) f -> e p k f", k=KD)[bass.DynSlice(e, 1)].rearrange("o p k f -> (o p) k f")
                    sp.dma_start(w13[par][:, :, i * FH:(i + 1) * FH], src).then_inc(s, 16)

            def load_w2(l, e, par):
                src = t["moe_w2"][l].rearrange("e (p k) n -> e p k n", k=2)[bass.DynSlice(e, 1)].rearrange("o p k n -> (o p) k n")
                sp.dma_start(w2s[par], src).then_inc(sem(f"exp2_{par}.{l}"), 16)

            def moe_loads(l):
                load_expert(l, 0, 0)
                load_w2(l, 0, 0)
                load_expert(l, 1, 1)
                load_w2(l, 1, 1)
                with sp.Fori(0, NE // 2 - 1) as i:
                    for par in range(2):
                        sp.wait_ge(sem(f"pe_h.{l}"), count(f"pe_h.{l}", i * 2 + par + 1))
                        load_expert(l, i * 2 + par + 2, par)
                        sp.wait_ge(sem(f"pe_o.{l}"), count(f"pe_o.{l}", i * 2 + par + 1))
                        load_w2(l, i * 2 + par + 2, par)
                sp.wait_ge(sem(f"over_ids.{l}"), count(f"over_ids.{l}", 1))
                for b in range(NE, NB):
                    e = sp.value_load(ovi[0:1, b - NE:b - NE + 1], min_val=0, max_val=NE - 1)
                    sp.wait_ge(sem(f"pe_h.{l}"), count(f"pe_h.{l}", b - 1))
                    load_expert(l, e, b % 2)
                    sp.wait_ge(sem(f"pe_o.{l}"), count(f"pe_o.{l}", b - 1))
                    load_w2(l, e, b % 2)

            sp.wait_ge(sem("pe_wo"), 4)
            moe_loads(0)
            sp.wait_ge(sem("pe_ada"), 4)
            for i in range(2):
                sp.dma_start(wq[i], dsa_in[:, :, OFF_Q + i * 512:OFF_Q + (i + 1) * 512]).then_inc(sem("wq_in"), 16)
            sp.wait_ge(sem("x_up.2"), count("x_up.2", NT))
            sp.dma_start(wqi, dsa_in[:, :, OFF_QI:OFF_QI + 512]).then_inc(sem("wqi_in"), 16)
            for i in range(2):
                sp.dma_start(kiw[:, :, i * HD:(i + 1) * HD], dsa_in[:, :, OFF_KI:OFF_KI + HD]).then_inc(sem("wqi_in"), 16)
                sp.dma_start(qkw[i * HD:(i + 1) * HD, 0:1], t["dsa_q_norm"].rearrange("o (d a) -> d (o a)", a=1)).then_inc(sem("wqi_in"), 16)
                sp.dma_start(qkw[i * HD:(i + 1) * HD, 1:2], t["dsa_k_norm"].rearrange("o (d a) -> d (o a)", a=1)).then_inc(sem("wqi_in"), 16)
            sp.dma_start(wiw, dsa_in[:, :, OFF_WI:OFF_WI + IH]).then_inc(sem("wqi_in"), 16)
            sp.dma_start(wkv, dsa_in[:, :, OFF_K:OFF_K + 512]).then_inc(sem("wkv_in"), 16)
            sp.wait_ge(sem("pe_qkv"), NT)
            sp.dma_start(wo_dsa, t["dsa_w_out"][0].rearrange("(c p) n -> p c n", p=P)).then_inc(sem("wo_dsa_in"), 16)
            moe_loads(1)
            for i in range(NT):
                sp.wait_ge(sem("x_up.4"), count("x_up.4", i + 1))
                sp.dma_start(t["out"][0, i * P:(i + 1) * P, :], x[:, i, :]).then_inc(sem("out_stored"), 16)
            sp.wait_ge(sem("out_stored"), 16 * NT)

        @block.gpsimd
        def _(pool):
            credit(pool, [n for n in CREDIT if n[0] == "p" and n[1] == "_"])
            def mask(tile, inside, fill, op, step):
                pool.memset(tile[:], inside)
                pool.drain()
                pool.affine_select(out=tile[:], in_=tile[:], compare_op=op, fill=fill, base=0,
                                   pattern=[[-step, P]], channel_multiplier=step)
            mask(ident, 0.0, 1.0, ALU.not_equal, 1)
            mask(upto, 1.0, 0.0, ALU.is_ge, -1)
            mask(after, 1.0, 0.0, ALU.is_gt, 1)
            mask(before, 1.0, 0.0, ALU.is_gt, -1)
            mask(causal, 0.0, NEG, ALU.is_ge, 1)
            pool.memset(ones[:], 1.0)
            pool.iota(iota[:], pattern=[[1, P]], base=0, channel_multiplier=0, allow_small_or_imprecise_dtypes=True)
            pool.iota(tokid[:], pattern=[[P, NT]], base=0, channel_multiplier=1, allow_small_or_imprecise_dtypes=True)
            pool.iota(pref[:], pattern=[[0, NT], [-1, 4]], base=4, channel_multiplier=0, allow_small_or_imprecise_dtypes=True)
            pool.memset(expo[:], -0.5)
            pool.memset(epst[:], EPS)
            for i in range(2):
                pool.memset(upad[i][:, 0:3], 0.0)
            pool.drain().then_inc(sem("consts"), 1)

            def norm(i):
                pool.wait_ge(sem(f"n_sq.{i}"), count(f"n_sq.{i}", NT))
                pool.tensor_scalar(rstd[:, i], ssq[:, i], 1.0 / D, EPS, ALU.mult, ALU.add)
                pool.drain()
                pool.tensor_tensor(rstd[:, i], rstd[:, i], expo[:, 0:NT], ALU.pow).then_inc(sem(f"n_rs.{i}"), 1)

            norm(0)

            def params(gn, par):
                pool.tensor_copy(gp[par][:, 0:2, :], cwT[:, :, bass.DynSlice(gn * 2, 2)].rearrange("p a c -> p c a"))
                pool.tensor_copy(gp[par][:, 2:3, :], cwT[:, :, bass.DynSlice(gn + CT, 1)].rearrange("p a c -> p c a"))
                pool.tensor_copy(gp[par][:, 3:4, :], cwT[:, :, bass.DynSlice(gn + CT + G, 1)].rearrange("p a c -> p c a"))
                pool.tensor_copy(gn_w[par], nwT[:, bass.DynSlice(gn * 2, 2)])
                pool.drain().then_inc(sem("p_gp"), 1)

            def triangle(g, j, m):
                if due(m - 1):
                    pool.wait_ge(sem("pe_df"), count("pe_df", m - 1))
                pool.tensor_tensor(tria[j % 2], rep(upto[:], JH), bc(aa[:, j, bass.DynSlice(g * JH, JH)], P),
                                   ALU.mult).then_inc(sem("p_tri"), 1)

            pool.wait_ge(sem("d_par"), 1)
            params(0, 0)
            pool.wait_ge(sem("d_dt"), 1)
            triangle(0, 0, 0)

            def step(g, j, par, last):
                m = g * NT + j
                if not (last and j == NT - 1):
                    if j < NT - 1:
                        triangle(g, j + 1, m + 1)
                    else:
                        triangle(g + 1, 0, m + 1)
                if j < NT - 1:
                    pool.wait_ge(sem("d_xdt"), m + 1)
                    if due(g * (NT - 1) + j):
                        pool.wait_ge(sem("pe_st"), count("pe_st", g * (NT - 1) + j))
                    pool.tensor_tensor(xd.rearrange("p (h d) -> p h d", d=HD), xdt.rearrange("p (h d) -> p h d", d=HD),
                                       bc(dte[:, j, bass.DynSlice(g * JH, JH)], HD), ALU.mult).then_inc(sem("p_xd"), 1)
                pool.wait_ge(sem("d_y"), count("d_y", m + 1))
                pool.wait_ge(sem("d_zs"), m + 1)
                pool.tensor_tensor(yb, yb, skip, ALU.add)
                pool.drain()
                pool.tensor_tensor(yb, yb, zs[par][:, j], ALU.mult).then_inc(sem("p_y"), 1)
                pool.wait_ge(sem("a_sq"), m + 1)
                pool.tensor_tensor(yrs, yss, epst[:], ALU.add)
                pool.drain()
                pool.tensor_tensor(yrs, yrs, expo[:, 0:1], ALU.pow).then_inc(sem("p_rs"), 1)

            def group(g, par, last):
                if not last:
                    if due(g * NT):
                        pool.wait_ge(sem("a_ye"), count("a_ye", g * NT))
                    if due(g * NT):
                        pool.wait_ge(sem("d_mu"), count("d_mu", g * NT))
                    params(g + 1, 1 - par)
                for j in range(NT):
                    step(g, j, par, last)

            with pool.Fori(0, G // 2 - 1) as i:
                group(i * 2, 0, False)
                group(i * 2 + 1, 1, False)
            group(G - 2, 0, False)
            group(G - 1, 1, True)

            def gate(i, col, s):
                for k in range(KD):
                    if due(k):
                        pool.wait_ge(sem(f"pe_gate.{i}"), count(f"pe_gate.{i}", k))
                    pool.tensor_scalar(s, ident[:], modcol[:, col, k:k + 1], None, ALU.mult).then_inc(sem(f"p_gate.{i}"), 1)

            pool.wait_ge(sem("d_ad"), count("d_ad", 1))
            gate(0, 2, diag0)

            def moe(l):
                norm(1 + 2 * l)
                pool.wait_ge(sem(f"n_xn.{1 + 2 * l}"), count(f"n_xn.{1 + 2 * l}", NT))
                gate(1 + 2 * l, 5 + 6 * l, mdiag)
                pool.wait_ge(sem(f"xn_stored.{l}"), count(f"xn_stored.{l}", 16))
                pool.wait_ge(sem(f"d_idx.{l}"), count(f"d_idx.{l}", 1))
                for b in range(NB):
                    if due(2 * (b - 1)):
                        pool.wait_ge(sem(f"pe_t.{l}"), count(f"pe_t.{l}", 2 * (b - 1)))
                    pool.indirect_dma_start(xg[b % 2], None, xn_dram[l],
                                            bass.IndirectOffsetOnAxis(ap=idx[:, b:b + 1], axis=0)).then_inc(sem(f"gath_{b % 2}.{l}"), 16)
                for i in range(2):
                    pool.wait_ge(sem(f"y_stored_{i}.{l}"), count(f"y_stored_{i}.{l}", 16 * ((NB + 1 - i) // 2)))
                for tt in range(NT):
                    if due(tt - 1):
                        pool.wait_ge(sem(f"x_up.{2 + 2 * l}"), count(f"x_up.{2 + 2 * l}", tt - 1))
                    for c in range(2):
                        pool.indirect_dma_start(yg[tt % 2][c], None, y_dram[l],
                                                bass.IndirectOffsetOnAxis(ap=sloti[:, c, tt:tt + 1], axis=0)
                                                ).then_inc(sem(f"yg_{tt % 2}.{l}"), 16)

            moe(0)
            norm(2)
            pool.wait_ge(sem("n_xn.2"), count("n_xn.2", NT))
            gate(2, 8, adiag)
            for tt in range(NT):
                pool.wait_ge(sem("d_hss"), tt + 1)
                pool.tensor_scalar(hrs, hss, 1.0 / HD, EPS, ALU.mult, ALU.add)
                pool.drain()
                pool.tensor_tensor(hrs, hrs, expo[:], ALU.pow).then_inc(sem("p_hrs"), 1)
            moe(1)

        @block.tensor
        def _(pe):
            credit(pe, [n for n in CREDIT if n[:2] == "pe"])
            def mm(out, lhsT, rhs, k, n):
                return pe.matmul(out, lhsT, rhs, start=(k == 0), stop=(k == n - 1))

            def ada_columns(buf, cols):
                for k1 in cols:
                    for k in range(KD):
                        last = mm(bank[7][:, GC + k1:GC + k1 + 1], buf[:, k, k1:D:KD], cond[:, k:k + 1], k, KD)
                return last

            def norm(i):
                pe.wait_ge(sem(f"n_xn.{i}"), count(f"n_xn.{i}", NT))
                for k in range(KD):
                    if k >= 2:
                        pe.wait_ge(sem(f"n_ev{k % 2}.{i}"), count(f"n_ev{k % 2}.{i}", k // 2))
                    for tt in range(NT):
                        last = pe.transpose(bank[k % 2][:, tt * P:(tt + 1) * P], xn[:, tt, k:D:KD], ident[:])
                    last.then_inc(sem(f"n_tr.{i}"), 1)

            def hT_ready(i):
                pe.wait_ge(sem(f"n_ev0.{i}"), count(f"n_ev0.{i}", KD // 2))
                pe.wait_ge(sem(f"n_ev1.{i}"), count(f"n_ev1.{i}", KD // 2))

            def gate(i, banks):
                for k in range(KD):
                    pe.wait_ge(sem(f"p_gate.{i}"), count(f"p_gate.{i}", k + 1))
                    pe.matmul(bank[banks[k // 4]][:, (k % 4) * P:(k % 4 + 1) * P], ones[:],
                              {0: diag0, 1: mdiag, 2: adiag, 3: mdiag}[i], start=True, stop=True
                              ).then_inc(sem(f"pe_gate.{i}"), 1)

            pe.wait_ge(sem("consts"), 1)
            pe.wait_ge(sem("cond"), 1)
            pe.wait_ge(sem("ada_in0"), 16)
            ada_columns(ada[0], range(KD)).then_inc(sem("pe_ada"), 1)
            pe.wait_ge(sem("ada_in1"), 16)
            pe.wait_ge(sem("d_ada"), 1)
            ada_columns(ada[1], range(KD)).then_inc(sem("pe_ada"), 1)
            pe.wait_ge(sem("par_in"), 160)
            pe.transpose(bank[2][:, 0:P], prow, ident[:])
            pe.transpose(bank[2][:, P:P + CONV_TILES + CT], brow[0:CONV_TILES + CT, :],
                         ident[0:CONV_TILES + CT, 0:CONV_TILES + CT]).then_inc(sem("pe_par"), 1)
            norm(0)
            hT_ready(0)
            for tt in range(NT):
                for k in range(KD):
                    last = mm(bank[3][:, tt * HEADS:(tt + 1) * HEADS], hT[:, k, tt * P:(tt + 1) * P], dtw[:, k], k, KD)
            last.then_inc(sem("pe_dt"), 1)

            def project_x(gn, par, j):
                n = gn * NT + j
                if due(n - 1):
                    pe.wait_ge(sem("a_xe"), n - 1)
                for k in range(KD):
                    last = mm(bank[j % 2][:], gw[par][:, k, j * P:(j + 1) * P], hT[:, k, :], k, KD)
                last.then_inc(sem("pe_x"), 1)

            def project_z(gn, par, j):
                n = gn * NT + j
                if due(n):
                    pe.wait_ge(sem("d_zs"), n)
                for k in range(KD):
                    last = mm(bank[2][:, 0:GC], hT[:, k, j * P:(j + 1) * P],
                              gw[par][:, k, 2 * GC:], k, KD)
                last.then_inc(sem("pe_z"), 1)

            def scan_in(g, par, j):
                m = g * NT + j
                if j == 0:
                    pe.wait_ge(sem("d_mu"), count("d_mu", g * NT + NT))
                cols = slice(j * P, (j + 1) * P)
                if due(m):
                    pe.wait_ge(sem("d_skip"), count("d_skip", m))
                if due(g * (NT - 1) + j):
                    pe.wait_ge(sem("d_bt"), count("d_bt", g * (NT - 1) + j))
                for i in range(3 if j < NT - 1 else 2):
                    last = pe.transpose(bank[3][:, i * P:(i + 1) * P], xbcT[par][:, i, cols], ident[:])
                last.then_inc(sem("pe_xt"), 1)
                if due(m):
                    pe.wait_ge(sem("d_cb"), count("d_cb", m))
                pe.matmul(bank[5][:, 0:P], xbcT[par][:, 2, cols], xbcT[par][:, 3, cols], start=True, stop=True
                          ).then_inc(sem("pe_cb"), 1)
                pe.wait_ge(sem("p_tri"), m + 1)
                if due(m):
                    pe.wait_ge(sem("a_ye"), count("a_ye", m))
                pe.matmul(bank[4][:], after[:], tria[j % 2].rearrange("p h l -> p (h l)"), start=True, stop=True
                          ).then_inc(sem("pe_df"), 1)

            def scan_out(g, par, j):
                m = g * NT + j
                if due(m):
                    pe.wait_ge(sem("d_y"), count("d_y", m))
                if j > 0:
                    if due(g * (NT - 1) + j):
                        pe.wait_ge(sem("d_st"), count("d_st", g * (NT - 1) + j))
                    pe.matmul(bank[6][:, GC:2 * GC], xbcT[par][:, 3, j * P:(j + 1) * P], state, start=True, stop=True)
                pe.wait_ge(sem("d_w"), count("d_w", m + 1))
                for h in range(JH):
                    last = pe.matmul(bank[6][:, h * HD:(h + 1) * HD], wmat[:, h, :], xdt[:, h * HD:(h + 1) * HD],
                                     start=True, stop=True)
                last.then_inc(sem("pe_y"), 1)
                if j < NT - 1:
                    pe.wait_ge(sem("p_xd"), g * (NT - 1) + j + 1)
                    pe.wait_ge(sem("d_bt"), count("d_bt", g * (NT - 1) + j + 1))
                    if due(g * (NT - 1) + j):
                        pe.wait_ge(sem("d_st"), count("d_st", g * (NT - 1) + j))
                    pe.matmul(bank[7][:, 0:GC], btok, xd, start=True, stop=True).then_inc(sem("pe_st"), 1)

            def turn_y(g, j):
                m = g * NT + j
                pe.wait_ge(sem("a_yn"), count("a_yn", m + 1))
                for i in range(2):
                    last = pe.transpose(bank[4][:, i * P:(i + 1) * P], yn[:, i * P:(i + 1) * P], ident[:])
                last.then_inc(sem("pe_yt"), 1)

            pe.wait_ge(sem("d_a"), 1)
            pe.matmul(bank[4][:, 0:P], upto[:], aa.rearrange("p c h -> p (c h)"), start=True, stop=True)
            pe.matmul(bank[4][:, P:2 * P], ones[:], aa.rearrange("p c h -> p (c h)"), start=True, stop=True
                      ).then_inc(sem("pe_cs"), 1)
            pe.wait_ge(sem("group_w0"), 64)
            pe.wait_ge(sem("d_par"), 1)
            for j in range(NT):
                project_x(0, 0, j)
                project_z(0, 0, j)
            pe.wait_ge(sem("d_dt"), 1)

            def group(g, par, last, even):
                for j in range(NT):
                    scan_in(g, par, j)
                    if not last:
                        if j == 0:
                            pe.wait_ge(sem(f"group_w{1 - par}"), even * 64 + (64 if par == 0 else 128))
                        project_x(g + 1, 1 - par, j)
                    scan_out(g, par, j)
                    if not last:
                        project_z(g + 1, 1 - par, j)
                    if j == 0:
                        pe.wait_ge(sem("ada_in0"), g * 16 + 32)
                        if due(g):
                            pe.wait_ge(sem("d_ad"), count("d_ad", g))
                    if due(g * (NT - 1) + min(j + 1, NT - 1)):
                        pe.wait_ge(sem("d_st"), count("d_st", g * (NT - 1) + min(j + 1, NT - 1)))
                    ada_columns(ada[0], (2 * j,))
                    turn_y(g, j)
                    ada_columns(ada[0], (2 * j + 1,)).then_inc(sem("pe_ad"), 1)

            pe.wait_ge(sem("d_ada"), 2)
            with pe.Fori(0, G // 2 - 1) as i:
                group(i * 2, 0, False, i)
                group(i * 2 + 1, 1, False, i)
            group(G - 2, 0, False, G // 2 - 1)
            group(G - 1, 1, True, G // 2 - 1)

            pe.wait_ge(sem("a_ye"), count("a_ye", G * NT))
            gate(0, (0, 1))
            pe.wait_ge(sem("ada_in0"), 16 * 10)
            pe.wait_ge(sem("d_ad"), count("d_ad", G))
            ada_columns(ada[0], range(KD)).then_inc(sem("pe_ada"), 1)
            pe.wait_ge(sem("d_gate.0"), count("d_gate.0", 2))
            pe.wait_ge(sem("d_ada"), 3)
            for c in range(CT):
                if c % 4 == 0:
                    pe.wait_ge(sem(f"wo_in{(c // 4) % 3}"), 16 * (c // 12 + 1))
                for tt in range(NT):
                    for hh in range(2):
                        last = mm(bank[2 * tt + hh][:], yT[:, c, tt * P:(tt + 1) * P],
                                  wo_ssd[(c // 4) % 3][:, c % 4, hh * 512:(hh + 1) * 512], c, CT)
                if c % 4 == 3:
                    last.then_inc(sem("pe_wo"), 1)

            def moe(l):
                i = 1 + 2 * l
                norm(i)
                gate(i, (2, 3))
                hT_ready(i)
                pe.wait_ge(sem(f"rt_in.{l}"), count(f"rt_in.{l}", 64))
                for tt in range(NT):
                    for k in range(KD):
                        last = mm(bank[4][:, tt * 20:(tt + 1) * 20], hT[:, k, tt * P:(tt + 1) * P], rtw[:, k], k, KD)
                last.then_inc(sem(f"pe_rt.{l}"), 1)
                pe.wait_ge(sem(f"d_m.{l}"), count(f"d_m.{l}", 1))
                m2 = MM.rearrange("p t e -> p (t e)")
                pe.matmul(bank[5][:, 0:NT * NE], before[:], m2, start=True, stop=True)
                pe.matmul(bank[5][:, NT * NE:2 * NT * NE], ones[:], m2, start=True, stop=True).then_inc(sem(f"pe_rank.{l}"), 1)
                pe.wait_ge(sem(f"d_r.{l}"), count(f"d_r.{l}", 1))
                for n in range(8):
                    last = mm(bank[6][:, 0:NB], R[n], Bm[:, n, :], n, 8)
                last.then_inc(sem(f"pe_idx.{l}"), 1)

                def turn_rows(b, par, n):
                    pe.wait_ge(sem(f"gath_{par}.{l}"), count(f"gath_{par}.{l}", n * 16 + 16))
                    for hh in range(2):
                        if due(b):
                            pe.wait_ge(sem(f"t_ev{hh}.{l}"), count(f"t_ev{hh}.{l}", b))
                        for k in range(4):
                            kk_ = hh * 4 + k
                            last = pe.transpose(bank[hh][:, k * P:(k + 1) * P], xg[par][:, kk_:D:KD], ident[:])
                        last.then_inc(sem(f"pe_t.{l}"), 1)

                def up(b, par, n):
                    pe.wait_ge(sem(f"t_ev0.{l}"), count(f"t_ev0.{l}", b + 1))
                    pe.wait_ge(sem(f"t_ev1.{l}"), count(f"t_ev1.{l}", b + 1))
                    pe.wait_ge(sem(f"exp13_{par}.{l}"), count(f"exp13_{par}.{l}", n * 32 + 32))
                    if due(b - 1):
                        pe.wait_ge(sem(f"d_hid.{l}"), count(f"d_hid.{l}", b - 1))
                    for k in range(KD):
                        last = mm(bank[2 + par][:], xgT[par][:, k, :], w13[par][:, k, :], k, KD)
                    last.then_inc(sem(f"pe_h.{l}"), 1)

                def turn_hidden(b, par):
                    pe.wait_ge(sem(f"d_hid.{l}"), count(f"d_hid.{l}", b + 1))
                    if due(b):
                        pe.wait_ge(sem(f"a_ht.{l}"), count(f"a_ht.{l}", b))
                    for k in range(2):
                        last = pe.transpose(bank[4][:, k * P:(k + 1) * P], hid[:, k:FH:2], ident[:])
                    last.then_inc(sem(f"pe_ht.{l}"), 1)

                def down(b, par, n):
                    pe.wait_ge(sem(f"a_ht.{l}"), count(f"a_ht.{l}", b + 1))
                    pe.wait_ge(sem(f"exp2_{par}.{l}"), count(f"exp2_{par}.{l}", n * 16 + 16))
                    if due(b):
                        pe.wait_ge(sem(f"a_yo.{l}"), count(f"a_yo.{l}", b))
                    if due(b):
                        pe.wait_ge(sem(f"d_yo.{l}"), count(f"d_yo.{l}", b))
                    for hh in range(2):
                        for k in range(2):
                            last = mm(bank[6 + hh][:], hidT[:, k, :], w2s[par][:, k, hh * 512:(hh + 1) * 512], k, 2)
                    last.then_inc(sem(f"pe_o.{l}"), 1)

                pe.wait_ge(sem(f"d_idx.{l}"), count(f"d_idx.{l}", 1))
                turn_rows(0, 0, 0)
                up(0, 0, 0)
                turn_rows(1, 1, 0)
                up(1, 1, 0)
                turn_rows(2, 0, 1)
                turn_hidden(0, 0)
                down(0, 0, 0)

                def two(i):
                    up(i * 2, 0, i)
                    turn_rows(i * 2 + 1, 1, i)
                    turn_hidden(i * 2 - 1, 1)
                    down(i * 2 - 1, 1, i - 1)
                    up(i * 2 + 1, 1, i)
                    turn_rows(i * 2 + 2, 0, i + 1)
                    turn_hidden(i * 2, 0)
                    down(i * 2, 0, i)
                with pe.Fori(1, NB // 2) as i:
                    two(i)
                up(NB - 1, 0, NB // 2)
                turn_hidden(NB - 2, 1)
                down(NB - 2, 1, NB // 2 - 1)
                turn_hidden(NB - 1, 0)
                down(NB - 1, 0, NB // 2)

            pe.wait_ge(sem("x_up.1"), count("x_up.1", NT))
            pe.wait_ge(sem("ada_in0"), 16 * 11)
            ada_columns(ada[0], range(KD)).then_inc(sem("pe_ada"), 1)
            moe(0)

            norm(2)
            gate(2, (2, 3))
            hT_ready(2)
            pe.wait_ge(sem("wqi_in"), 16 * 8)
            pe.wait_ge(sem("d_gate.2"), count("d_gate.2", 2))
            for j in range(5):
                if due(j - 1):
                    pe.wait_ge(sem("a_qi"), j - 1)
                for k in range(KD):
                    lw = wqi[:, k, j * P:(j + 1) * P] if j < 4 else kiw[:, k, :]
                    last = mm(bank[j % 2][:], lw, hT[:, k, :], k, KD)
                last.then_inc(sem("pe_qi"), 1)
            for tt in range(NT):
                for k in range(KD):
                    last = mm(bank[2][:, tt * IH:(tt + 1) * IH], hT[:, k, tt * P:(tt + 1) * P], wiw[:, k], k, KD)
            last.then_inc(sem("pe_wi"), 1)
            pe.wait_ge(sem("a_qi"), 5)
            n = 0
            for tt in range(1, NT):
                w = (tt + 1) * P
                for h in range(IH):
                    if due(n - 1):
                        pe.wait_ge(sem("a_rel"), n - 1)
                    rows = slice((h % 2) * HD, (h % 2 + 1) * HD)
                    pe.matmul(bank[6 + n % 2][:, 0:w], qiT[rows, h // 2, tt * P:(tt + 1) * P], kiT[rows, 0:w],
                              start=True, stop=True).then_inc(sem("pe_is"), 1)
                    n += 1
            pe.wait_ge(sem("wq_in"), 32)
            pe.wait_ge(sem("wkv_in"), 16)
            pe.wait_ge(sem("d_wi"), 1)
            pe.wait_ge(sem("a_rel"), 3 * IH)

            def turn_qk(tt):
                pe.wait_ge(sem("d_qkn"), tt + 1)
                for gi in range(3):
                    n = 3 * tt + gi
                    if due(n - 1):
                        pe.wait_ge(sem("qk_ev"), n - 1)
                    for i in range(4):
                        src = qkn[:, (gi * 4 + i) * P:(gi * 4 + i + 1) * P]
                        last = pe.transpose(bank[6 + n % 2][:, i * P:(i + 1) * P], src, ident[:])
                    last.then_inc(sem("pe_qk"), 1)

            for tt in range(NT):
                b0 = 3 * (tt % 2)
                if due(tt - 1):
                    pe.wait_ge(sem("d_qkn"), tt - 1)
                if due(tt - 1):
                    pe.wait_ge(sem("a_v"), tt - 1)
                for i in range(3):
                    for k in range(KD):
                        last = mm(bank[b0 + i][:], hT[:, k, tt * P:(tt + 1) * P], (wq[0], wq[1], wkv)[i][:, k, :], k, KD)
                last.then_inc(sem("pe_qkv"), 1)
                if tt > 0:
                    turn_qk(tt - 1)
            turn_qk(NT - 1)
            pe.wait_ge(sem("qk_ev"), 12)

            def scores(u):
                tt, kv = u // 4, u % 4
                w = (tt + 1) * P
                for i in range(4):
                    h = 4 * kv + i
                    rows = slice((h % 2) * HD, (h % 2 + 1) * HD)
                    if u > 0:
                        pe.wait_ge(sem("d_sm"), 4 * (u - 1) + i + 1)
                    pe.matmul(bank[i][:, 0:w], qT[rows, h // 2, tt * P:(tt + 1) * P], kT[rows, kv, 0:w],
                              start=True, stop=True).then_inc(sem("pe_s"), 1)

            def attend(u):
                tt, kv = u // 4, u % 4
                base = chunks_before(u)
                if u % 4 == 0:
                    if due(2 * tt):
                        pe.wait_ge(sem("d_xo"), 2 * tt)
                pe.wait_ge(sem("a_exp"), 4 * u + 4)
                for c in range(tt + 1):
                    n = base + c
                    if due(n - 1):
                        pe.wait_ge(sem("pt_ev"), n - 1)
                    for i in range(4):
                        last = pe.transpose(bank[4 + n % 2][:, i * P:(i + 1) * P], Sm[u % 2][:, i, c * P:(c + 1) * P], ident[:])
                    last.then_inc(sem("pe_pt"), 1)
                pe.wait_ge(sem("pt_ev"), base + tt + 1)
                for i in range(4):
                    h = 4 * kv + i
                    for c in range(tt + 1):
                        last = mm(bank[6 + h // 8][:, (h % 8) * HD:(h % 8 + 1) * HD], PT[:, c, i * P:(i + 1) * P],
                                  V[:, c, kv * HD:(kv + 1) * HD], c, tt + 1)
                last.then_inc(sem("pe_pv"), 1)

            def project_out(tt):
                pe.wait_ge(sem("d_o"), tt + 1)
                for hh in range(2):
                    for i in range(4):
                        last = pe.transpose(bank[4 + hh][:, i * P:(i + 1) * P],
                                            o[:, (hh * 4 + i) * P:(hh * 4 + i + 1) * P], ident[:])
                    last.then_inc(sem("pe_ot"), 1)
                pe.wait_ge(sem("ot_ev"), 2 * tt + 2)
                pe.wait_ge(sem("wo_dsa_in"), 16)
                for hh in range(2):
                    for k in range(KD):
                        last = mm(bank[6 + hh][:], oT[:, k, :], wo_dsa[:, k, hh * 512:(hh + 1) * 512], k, KD)
                    last.then_inc(sem("pe_xo"), 1)

            scores(0)
            for u in range(16):
                if u < 15:
                    scores(u + 1)
                attend(u)
                if u % 4 == 3:
                    project_out(u // 4)
            pe.wait_ge(sem("d_xo"), 8)
            moe(1)

        @block.scalar
        def _(act):
            credit(act, [n for n in CREDIT if n[0] == "a"])
            def copy(out, in_):
                return act.activation(out, in_, ACT.Copy)

            def squares(i):
                for tt in range(NT):
                    if i > 0:
                        act.wait_ge(sem("x_up"), (i - 1) * NT + tt + 1)
                    act.activation(xn[:, tt], x[:, tt], ACT.Square, accum_out=ssq[:, i, tt:tt + 1]).then_inc(sem(f"n_sq.{i}"), 1)

            def norm(i):
                act.wait_ge(sem(f"n_col.{i}"), count(f"n_col.{i}", 1))
                for k in range(1, KD, 2):
                    act.wait_ge(sem(f"n_tr.{i}"), count(f"n_tr.{i}", k + 1))
                    act.activation(hT[:, k, :], bank[1][:], ACT.Identity, bias=modcol[:, 3 * i, k:k + 1],
                                   scale=acol[:, i, k:k + 1]).then_inc(sem(f"n_ev1.{i}"), 1)

            act.wait_ge(sem("c_in"), 16)
            act.activation(cond[:], ccol[:], ACT.Tanh, scale=0.5).then_inc(sem("a_c"), 1)
            act.wait_ge(sem("x_in"), 16)
            squares(0)
            norm(0)
            act.wait_ge(sem("d_v"), 1)
            act.activation(s2, s2, ACT.Exp)
            act.activation(alog, alog, ACT.Exp).then_inc(sem("a_dt"), 1)
            act.wait_ge(sem("d_cs"), 1)
            act.activation(ea, acs, ACT.Exp)
            act.activation(dte, dte, ACT.Exp)
            act.activation(s3, s3, ACT.Exp)
            act.drain().then_inc(sem("a_dec"), 1)

            def conv_in(gn, par, j):
                n = gn * NT + j
                if j == 0:
                    act.wait_ge(sem("p_gp"), gn + 1)
                act.wait_ge(sem("pe_x"), n + 1)
                if due(n - 1):
                    act.wait_ge(sem("d_mu"), count("d_mu", n - 1))
                copy(upad[j % 2][:, 3:515], bank[j % 2][:])
                act.activation(cacc[j % 2], bank[j % 2][:], ACT.Identity, bias=gp[par][:, j, 4:5],
                               scale=gp[par][:, j, 3:4]).then_inc(sem("a_xe"), 1)

            def conv_tanh(gn, j):
                n = gn * NT + j
                act.wait_ge(sem("d_cv"), n + 1)
                act.activation(th[j % 2], cacc[j % 2], ACT.Tanh).then_inc(sem("a_th"), 1)

            def z_tanh(gn, j):
                n = gn * NT + j
                act.wait_ge(sem("pe_z"), n + 1)
                if due(n):
                    act.wait_ge(sem("d_zs"), n)
                act.activation(zt, bank[2][:, 0:GC], ACT.Tanh, scale=0.5).then_inc(sem("a_zt"), 1)

            for j in range(NT):
                conv_in(0, 0, j)
                z_tanh(0, j)
                conv_tanh(0, j)

            def group(g, par, last):
                for j in range(NT):
                    m = g * NT + j
                    act.wait_ge(sem("pe_df"), count("pe_df", m + 1))
                    if due(m):
                        act.wait_ge(sem("d_w"), count("d_w", m))
                    act.activation(decay.rearrange("p h l -> p (h l)"), bank[4][:], ACT.Exp).then_inc(sem("a_ex"), 1)
                    if not last:
                        conv_in(g + 1, 1 - par, j)
                    act.wait_ge(sem("p_y"), count("p_y", m + 1))
                    if due(m):
                        act.wait_ge(sem("pe_yt"), count("pe_yt", m))
                    act.activation(yn, yb, ACT.Square, scale=0.5 * GC ** -0.5, accum_out=yss).then_inc(sem("a_sq"), 1)
                    if not last:
                        z_tanh(g + 1, j)
                        conv_tanh(g + 1, j)
                    act.wait_ge(sem("p_rs"), m + 1)
                    act.activation(yn, yb, ACT.Copy, scale=yrs).then_inc(sem("a_yn"), 1)
                    act.wait_ge(sem("pe_yt"), count("pe_yt", m + 1))
                    for i in range(2):
                        ins = act.activation(yT[:, bass.DynSlice(g * 2 + i, 1), j * P:(j + 1) * P],
                                             bank[4][:, i * P:(i + 1) * P].unsqueeze(1), ACT.Copy,
                                             scale=gn_w[par][:, i:i + 1])
                    act.drain().then_inc(sem("a_ye"), 1)

            with act.Fori(0, G // 2 - 1) as i:
                group(i * 2, 0, False)
                group(i * 2 + 1, 1, False)
            group(G - 2, 0, False)
            group(G - 1, 1, True)

            def moe(l):
                i = 1 + 2 * l
                squares(i)
                act.wait_ge(sem(f"x_up.{i}"), count(f"x_up.{i}", NT))
                s = sem(f"rt_in.{l}")
                act.dma_start(rtw[:, :, 0:NG], t["moe_w_group"][l].rearrange("(p k) n -> p k n", k=KD)).then_inc(s, 16)
                act.dma_start(rtw[:, :, NG:], t["moe_w_expert"][l].rearrange("(p k) n -> p k n", k=KD)).then_inc(s, 16)
                act.dma_start(rtb[:, 0:NG], row_bc(t["moe_b_group"][l], NG)).then_inc(s, 16)
                act.dma_start(rtb[:, NG:], row_bc(t["moe_b_expert"][l], NE)).then_inc(s, 16)
                act.wait_ge(sem(f"n_xn.{i}"), count(f"n_xn.{i}", NT))
                act.dma_start(xn_dram[l].rearrange("(t p) d -> p t d", p=P), xn[:]).then_inc(sem(f"xn_stored.{l}"), 16)
                norm(i)
                act.wait_ge(sem(f"d_g.{l}"), count(f"d_g.{l}", 1))
                act.activation(gsh, gsh, ACT.Exp).then_inc(sem(f"a_r.{l}"), 1)
                act.wait_ge(sem(f"d_e.{l}"), count(f"d_e.{l}", 1))
                act.activation(g2, g2, ACT.Exp).then_inc(sem(f"a_r.{l}"), 1)

                def turned(b, par):
                    act.wait_ge(sem(f"pe_t.{l}"), count(f"pe_t.{l}", b * 2 + 2))
                    if due(b - 1):
                        act.wait_ge(sem(f"pe_h.{l}"), count(f"pe_h.{l}", b - 1))
                    for k in range(4):
                        act.activation(xgT[par][:, 4 + k, :], bank[1][:, k * P:(k + 1) * P], ACT.Identity,
                                       bias=modcol[:, 3 * i, 4 + k:5 + k], scale=acol[:, i, 4 + k:5 + k])
                    act.drain().then_inc(sem(f"t_ev1.{l}"), 1)

                def gate_tanh(b, par):
                    act.wait_ge(sem(f"pe_h.{l}"), count(f"pe_h.{l}", b + 1))
                    if due(b):
                        act.wait_ge(sem(f"d_hid.{l}"), count(f"d_hid.{l}", b))
                    act.activation(mth, bank[2 + par][:, 0:FH], ACT.Tanh, scale=0.5).then_inc(sem(f"a_mt.{l}"), 1)

                def hidden_turned(b):
                    act.wait_ge(sem(f"pe_ht.{l}"), count(f"pe_ht.{l}", b + 1))
                    if due(b):
                        act.wait_ge(sem(f"pe_o.{l}"), count(f"pe_o.{l}", b))
                    copy(hidT.rearrange("p a b -> p (a b)"), bank[4][:, 0:2 * P]).then_inc(sem(f"a_ht.{l}"), 1)

                def result(b, par, n):
                    act.wait_ge(sem(f"pe_o.{l}"), count(f"pe_o.{l}", b + 1))
                    if due(n * 16):
                        act.wait_ge(sem(f"y_stored_{par}.{l}"), count(f"y_stored_{par}.{l}", n * 16))
                    copy(yo[par][:, 0:512], bank[6][:]).then_inc(sem(f"a_yo.{l}"), 1)
                    act.wait_ge(sem(f"d_yo.{l}"), count(f"d_yo.{l}", b + 1))
                    act.wait_ge(sem(f"a_yo.{l}"), count(f"a_yo.{l}", b + 1))
                    act.dma_start(y_dram[l].rearrange("(b p) d -> b p d", p=P)[bass.DynSlice(b, 1)].rearrange("o p d -> (o p) d"),
                                  yo[par]).then_inc(sem(f"y_stored_{par}.{l}"), 16)

                act.wait_ge(sem(f"d_idx.{l}"), count(f"d_idx.{l}", 1))
                turned(0, 0)
                gate_tanh(0, 0)
                turned(1, 1)
                gate_tanh(1, 1)
                turned(2, 0)
                hidden_turned(0)
                result(0, 0, 0)
                with act.Fori(1, NB // 2) as ii:
                    gate_tanh(ii * 2, 0)
                    turned(ii * 2 + 1, 1)
                    hidden_turned(ii * 2 - 1)
                    result(ii * 2 - 1, 1, ii - 1)
                    gate_tanh(ii * 2 + 1, 1)
                    turned(ii * 2 + 2, 0)
                    hidden_turned(ii * 2)
                    result(ii * 2, 0, ii)
                gate_tanh(NB - 1, 0)
                hidden_turned(NB - 2)
                result(NB - 2, 1, NB // 2 - 1)
                hidden_turned(NB - 1)
                result(NB - 1, 0, NB // 2)

            moe(0)

            squares(2)
            norm(2)
            for j in range(5):
                act.wait_ge(sem("pe_qi"), j + 1)
                copy(qiT[:, j, :] if j < 4 else kiT, bank[j % 2][:]).then_inc(sem("a_qi"), 1)
            n = 0
            for tt in range(1, NT):
                w = (tt + 1) * P
                for h in range(IH):
                    act.wait_ge(sem("pe_is"), n + 1)
                    if due(n - 1):
                        act.wait_ge(sem("d_acc"), n - 1)
                    act.activation(rel[n % 2][:, 0:w], bank[6 + n % 2][:, 0:w], ACT.Relu, scale=HD ** -0.5).then_inc(sem("a_rel"), 1)
                    n += 1

            def turned_qk(tt):
                for gi in (0, 1, 2):
                    n = 3 * tt + gi
                    act.wait_ge(sem("pe_qk"), n + 1)
                    dst = qT[:, 4 * gi:4 * gi + 4, tt * P:(tt + 1) * P] if gi < 2 else kT[:, :, tt * P:(tt + 1) * P]
                    act.activation(dst, bank[6 + n % 2][:].rearrange("p (a b) -> p a b", b=P), ACT.Copy,
                                   scale=qkw[:, gi // 2:gi // 2 + 1]).then_inc(sem("qk_ev"), 1)

            for tt in range(NT):
                b0 = 3 * (tt % 2)
                act.wait_ge(sem("pe_qkv"), tt + 1)
                if due(tt):
                    act.wait_ge(sem("d_hss"), tt)
                act.activation(sqs[:, 0:512], bank[b0][:], ACT.Square)
                act.activation(sqs[:, 512:1024], bank[b0 + 1][:], ACT.Square)
                act.activation(sqs[:, 1024:1280], bank[b0 + 2][:, 0:256], ACT.Square)
                copy(V[:, tt, :], bank[b0 + 2][:, 256:512]).then_inc(sem("a_v"), 1)
                act.drain().then_inc(sem("a_sqs"), 1)
                if tt > 0:
                    turned_qk(tt - 1)
            turned_qk(NT - 1)
            for u in range(16):
                tt, kv = u // 4, u % 4
                w = (tt + 1) * P
                base = chunks_before(u)
                act.wait_ge(sem("d_nmx"), u + 1)
                for i in range(4):
                    act.activation(Sm[u % 2][:, i, 0:w], Sm[u % 2][:, i, 0:w], ACT.Exp, bias=nmx[:, kv, i:i + 1],
                                   accum_out=rsum[:, 4 * kv + i:4 * kv + i + 1]).then_inc(sem("a_exp"), 1)
                for c in range(tt + 1):
                    act.wait_ge(sem("pe_pt"), base + c + 1)
                    if due(u):
                        act.wait_ge(sem("pe_pv"), u)
                    copy(PT[:, c, :], bank[4 + (base + c) % 2][:]).then_inc(sem("pt_ev"), 1)
                if kv == 3:
                    for hh in range(2):
                        act.wait_ge(sem("pe_ot"), 2 * tt + hh + 1)
                        copy(oT[:, 4 * hh:4 * hh + 4, :].rearrange("p a b -> p (a b)"), bank[4 + hh][:]).then_inc(sem("ot_ev"), 1)
            moe(1)

        @block.vector
        def _(dve):
            credit(dve, [n for n in CREDIT if n[0] == "d"])
            def tt_(out, a, b, op):
                dve.tensor_tensor(out, a, b, op)
                dve.drain()

            def ts_(out, a, s1_, s2_, op0, op1=ALU.bypass):
                if s2_ is None:
                    dve.tensor_scalar(out, a, s1_, None, op0)
                else:
                    dve.tensor_scalar(out, a, s1_, s2_, op0, op1)
                dve.drain()

            def stt(out, a, s, b, op0, op1):
                return dve.scalar_tensor_tensor(out=out, in0=a, scalar=s, in1=b, op0=op0, op1=op1)

            def red(out, a, op):
                dve.tensor_reduce(out, a, AX.X, op)
                dve.drain()

            def ada_out(i, s):
                return dve.tensor_tensor(modcol[:, i, :], bank[7][:, GC:GC + KD], adab[:, i, :], ALU.add).then_inc(s, 1)

            def norm(i):
                dve.wait_ge(sem(f"n_rs.{i}"), count(f"n_rs.{i}", 1))
                for tt in range(NT):
                    dve.tensor_scalar(xn[:, tt], x[:, tt], rstd[:, i, tt:tt + 1], None, ALU.mult).then_inc(sem(f"n_xn.{i}"), 1)
                if i == 0:
                    for n in range(2):
                        if n == 0:
                            dve.wait_ge(sem("par_in"), 160)
                        dve.wait_ge(sem("pe_ada"), n + 1)
                        ada_out(n, sem("d_ada"))
                dve.drain()
                stt(acol[:, i], modcol[:, 3 * i + 1], 1.0, normw[:, i], ALU.add, ALU.mult).then_inc(sem(f"n_col.{i}"), 1)
                dve.drain()
                for k in range(0, KD, 2):
                    dve.wait_ge(sem(f"n_tr.{i}"), count(f"n_tr.{i}", k + 1))
                    dve.tensor_scalar(hT[:, k, :], bank[0][:], acol[:, i, k:k + 1], modcol[:, 3 * i, k:k + 1],
                                      ALU.mult, ALU.add).then_inc(sem(f"n_ev0.{i}"), 1)

            def gate(i, banks, dst):
                for hh in range(2):
                    dve.wait_ge(sem(f"pe_gate.{i}"), count(f"pe_gate.{i}", 4 * hh + 4))
                    dve.tensor_copy(dst.rearrange("p (q k) -> p k q", k=KD)[:, 4 * hh:4 * hh + 4, :],
                                    bank[banks[hh]][:].rearrange("p (k q) -> p k q", k=4)).then_inc(sem(f"d_gate.{i}"), 1)

            dve.wait_ge(sem("a_c"), 1)
            stt(cond[:], cond[:], 1.0, ccol[:], ALU.add, ALU.mult)
            dve.drain()
            dve.tensor_scalar(cond[:], cond[:], 0.5, None, ALU.mult).then_inc(sem("cond"), 1)
            norm(0)
            dve.wait_ge(sem("pe_par"), 1)
            dve.tensor_scalar(cwT.rearrange("p a c -> p (a c)"), bank[2][:, 0:160], 0.5, None, ALU.mult)
            dve.tensor_scalar(nwT, bank[2][:, 160:160 + CT], 0.5, None, ALU.mult)
            dve.drain().then_inc(sem("d_par"), 1)
            dve.wait_ge(sem("pe_dt"), 1)
            tt_(s1, bank[3][:, 0:P].rearrange("p (c h) -> p c h", h=HEADS), rep(dtb, NT), ALU.add)
            ts_(s3, s1, -1.0, None, ALU.mult)
            dve.tensor_tensor(s2, s1, s3, ALU.min).then_inc(sem("d_v"), 1)
            ts_(s1, s1, 0.0, None, ALU.max)
            dve.wait_ge(sem("a_dt"), 1)
            ts_(s3, s2, 2.0, None, ALU.add)
            dve.reciprocal(s3, s3)
            dve.drain()
            tt_(s2, s2, s3, ALU.mult)
            tt_(s3, s2, s2, ALU.mult)
            ts_(dt, s3, 1.0 / (2 * LOG1P_TERMS + 1), 1.0 / (2 * LOG1P_TERMS - 1), ALU.mult, ALU.add)
            for n in range(LOG1P_TERMS - 2, -1, -1):
                tt_(dt, dt, s3, ALU.mult)
                ts_(dt, dt, 1.0 / (2 * n + 1), None, ALU.add)
            tt_(dt, dt, s2, ALU.mult)
            stt(dt, dt, 2.0, s1, ALU.mult, ALU.add)
            dve.drain()
            stt(aa, dt, -1.0, rep(alog, NT), ALU.mult, ALU.mult).then_inc(sem("d_a"), 1)
            dve.wait_ge(sem("pe_cs"), 1)
            a2 = bank[4][:, 0:P].rearrange("p (c h) -> p c h", h=HEADS)
            last2 = bank[4][:, P:2 * P].rearrange("p (c h) -> p c h", h=HEADS)
            dve.tensor_copy(acs, a2)
            dve.tensor_copy(s3, last2)
            dve.drain()
            dve.tensor_tensor(dte, s3, acs, ALU.subtract)
            dve.drain().then_inc(sem("d_cs"), 1)
            dve.wait_ge(sem("a_dec"), 1)
            dve.drain().then_inc(sem("d_dt"), 1)

            def conv(gn, par, j):
                n = gn * NT + j
                dve.wait_ge(sem("a_xe"), n + 1)
                for k in range(3):
                    ins = stt(cacc[j % 2], upad[j % 2][:, k:k + SEQ], gp[par][:, j, k:k + 1], cacc[j % 2], ALU.mult, ALU.add)
                    if k < 2:
                        dve.drain()
                ins.then_inc(sem("d_cv"), 1)

            def conv_silu(gn, par, j):
                n = gn * NT + j
                dve.wait_ge(sem("a_th"), n + 1)
                stt(xbcT[par][:, j, :], th[j % 2], 1.0, cacc[j % 2], ALU.add, ALU.mult).then_inc(sem("d_mu"), 1)

            def z_silu(gn, par, j):
                n = gn * NT + j
                dve.wait_ge(sem("a_zt"), n + 1)
                stt(zs[par][:, j], zt, 1.0, bank[2][:, 0:GC], ALU.add, ALU.mult).then_inc(sem("d_zs"), 1)

            for j in range(NT):
                conv(0, 0, j)
                z_silu(0, 0, j)
                conv_silu(0, 0, j)

            def heads(ap):
                return ap.rearrange("p (h d) -> p h d", d=HD)

            def group(g, par, last):
                hs = bass.DynSlice(g * JH, JH)
                for j in range(NT):
                    m = g * NT + j
                    dve.wait_ge(sem("pe_xt"), m + 1)
                    dve.tensor_tensor(heads(xdt), heads(bank[3][:, 0:GC]), bc(dt[:, j, hs], HD), ALU.mult).then_inc(sem("d_xdt"), 1)
                    if due(m):
                        dve.wait_ge(sem("p_y"), count("p_y", m))
                    dve.tensor_tensor(heads(skip), heads(bank[3][:, 0:GC]), bc(dsk[:, hs], HD), ALU.mult).then_inc(sem("d_skip"), 1)
                    if j < NT - 1:
                        if due(g * (NT - 1) + j):
                            dve.wait_ge(sem("pe_st"), count("pe_st", g * (NT - 1) + j))
                        dve.tensor_copy(btok, bank[3][:, 2 * P:3 * P]).then_inc(sem("d_bt"), 1)
                    dve.wait_ge(sem("pe_cb"), m + 1)
                    dve.tensor_tensor(cbm, bank[5][:, 0:P], upto[:], ALU.mult).then_inc(sem("d_cb"), 1)
                    dve.drain()
                    dve.wait_ge(sem("a_ex"), m + 1)
                    dve.tensor_tensor(wmat, decay, rep(cbm, JH), ALU.mult).then_inc(sem("d_w"), 1)
                    dve.wait_ge(sem("pe_y"), m + 1)
                    if due(m):
                        dve.wait_ge(sem("a_yn"), count("a_yn", m))
                    if j == 0:
                        dve.tensor_copy(yb, bank[6][:, 0:GC]).then_inc(sem("d_y"), 1)
                    else:
                        dve.tensor_tensor(heads(yb), heads(bank[6][:, GC:2 * GC]), bc(ea[:, j, hs], HD), ALU.mult)
                        dve.drain()
                        dve.tensor_tensor(yb, yb, bank[6][:, 0:GC], ALU.add).then_inc(sem("d_y"), 1)
                    if j == 0:
                        dve.wait_ge(sem("pe_st"), count("pe_st", g * (NT - 1) + j + 1))
                        dve.tensor_copy(state, bank[7][:, 0:GC]).then_inc(sem("d_st"), 1)
                    elif j < NT - 1:
                        dve.tensor_tensor(heads(state), heads(state), bc(s3[:, j, hs], HD), ALU.mult)
                        dve.drain()
                        dve.wait_ge(sem("pe_st"), count("pe_st", g * (NT - 1) + j + 1))
                        dve.tensor_tensor(state, state, bank[7][:, 0:GC], ALU.add).then_inc(sem("d_st"), 1)
                    if not last:
                        conv(g + 1, 1 - par, j)
                        z_silu(g + 1, 1 - par, j)
                        conv_silu(g + 1, 1 - par, j)
                dve.wait_ge(sem("pe_ad"), g * NT + NT)
                dve.tensor_tensor(modcol[:, bass.DynSlice(g + 2, 1), :], bank[7][:, GC:GC + KD].unsqueeze(1),
                                  adab[:, bass.DynSlice(g + 2, 1), :], ALU.add).then_inc(sem("d_ad"), 1)

            with dve.Fori(0, G // 2 - 1) as i:
                group(i * 2, 0, False)
                group(i * 2 + 1, 1, False)
            group(G - 2, 0, False)
            group(G - 1, 1, True)
            gate(0, (0, 1), gatebc0)
            dve.wait_ge(sem("pe_ada"), 3)
            ada_out(10, sem("d_ada"))
            dve.drain()
            dve.wait_ge(sem("pe_wo"), 4)
            for tt in range(NT):
                for hh in range(2):
                    half = slice(hh * 512, (hh + 1) * 512)
                    dve.tensor_tensor(xn[:, tt, half], bank[2 * tt + hh][:], gatebc0[:, half], ALU.mult)
                dve.drain()
                dve.tensor_tensor(x[:, tt], x[:, tt], xn[:, tt], ALU.add).then_inc(sem("x_up.1"), 1)

            def onehot(dst, vals, mx):
                red(mx, vals, ALU.max)
                tt_(cand, vals, bc(mx, 4), ALU.is_equal)
                tt_(cand, cand, pref[:], ALU.mult)
                red(g3, cand, ALU.max)
                tt_(dst, cand, bc(g3, 4), ALU.is_equal)

            def moe(l):
                i = 1 + 2 * l
                if l == 0:
                    dve.wait_ge(sem("pe_ada"), 4)
                    ada_out(11, sem("d_ada"))
                norm(i)
                gate(i, (2, 3), gatebc)
                dve.wait_ge(sem(f"pe_rt.{l}"), count(f"pe_rt.{l}", 1))
                dve.wait_ge(sem(f"rt_in.{l}"), count(f"rt_in.{l}", 64))
                tt_(lg, bank[4][:, 0:80].rearrange("p (t e) -> p t e", e=20), rep(rtb, NT), ALU.add)
                onehot(goh, lg[:, :, 0:NG], mx1)
                dve.tensor_tensor(gsh, lg[:, :, 0:NG], bc(mx1, 4), ALU.subtract).then_inc(sem(f"d_g.{l}"), 1)
                for g in range(NG):
                    dve.tensor_tensor(prod[:, :, g * EG:(g + 1) * EG], lg[:, :, NG + g * EG:NG + (g + 1) * EG],
                                      bc(goh[:, :, g], EG), ALU.mult)
                dve.drain()
                tt_(ein, prod[:, :, 0:4], prod[:, :, 4:8], ALU.add)
                tt_(ein, ein, prod[:, :, 8:12], ALU.add)
                tt_(ein, ein, prod[:, :, 12:16], ALU.add)
                onehot(oh1, ein, mx1)
                stt(m4, oh1, NEG, ein, ALU.mult, ALU.add)
                dve.drain()
                onehot(oh2, m4, mx2)
                dve.tensor_tensor(g2, mx2, mx1, ALU.subtract).then_inc(sem(f"d_e.{l}"), 1)
                for g in range(NG):
                    dve.tensor_tensor(M1[:, :, g * EG:(g + 1) * EG], oh1, bc(goh[:, :, g], EG), ALU.mult)
                    dve.tensor_tensor(M2[:, :, g * EG:(g + 1) * EG], oh2, bc(goh[:, :, g], EG), ALU.mult)
                dve.drain()
                dve.tensor_tensor(MM, M1, M2, ALU.add).then_inc(sem(f"d_m.{l}"), 1)
                dve.wait_ge(sem(f"a_r.{l}"), count(f"a_r.{l}", 2))
                red(g1, gsh, ALU.add)
                ts_(g3, g2, 1.0, None, ALU.add)
                tt_(g1, g1, g3, ALU.mult)
                dve.reciprocal(g1, g1)
                dve.drain()
                ts_(wc1, g1, 0.5, None, ALU.mult)
                tt_(wc2, wc1, g2, ALU.mult)
                dve.wait_ge(sem(f"pe_rank.{l}"), count(f"pe_rank.{l}", 1))
                cnt = bank[5][:, NT * NE:2 * NT * NE].rearrange("p (t e) -> p t e", e=NE)
                dve.memset(toff[:, 0], 0.0)
                dve.drain()
                for tt in range(1, NT):
                    tt_(toff[:, tt], toff[:, tt - 1], cnt[:, tt - 1], ALU.add)
                tt_(tot, toff[:, NT - 1], cnt[:, NT - 1], ALU.add)
                tt_(rank, toff, bank[5][:, 0:NT * NE].rearrange("p (t e) -> p t e", e=NE), ALU.add)
                ts_(over, tot, float(P), None, ALU.is_gt)
                for c in (2, 3):
                    stt(over, tot, float(c * P), over, ALU.is_gt, ALU.add)
                    dve.drain()
                dve.tensor_tensor_scan(cumi, ones[:, 0:NE], over, 0.0, ALU.mult, ALU.add)
                dve.drain()
                tt_(base2, cumi, over, ALU.subtract)
                ts_(base2, base2, float(NE - 1), None, ALU.add)
                tt_(ovt[0:1], rep(cumi[0:1, :], OVER), bc(iota[0:1, 0:OVER], NE), ALU.is_le)
                red(ovf[0:1], ovt[0:1], ALU.add)
                ts_(ovf[0:1], ovf[0:1], float(NE - 1), None, ALU.min)
                dve.tensor_copy(ovi[0:1], ovf[0:1]).then_inc(sem(f"over_ids.{l}"), 1)
                for c, M in ((0, M1), (1, M2)):
                    tt_(prod, M, rank, ALU.mult)
                    red(rr[:, c], prod, ALU.add)
                    tt_(prod, M, rep(iota[:, 0:NE], NT), ALU.mult)
                    red(blk[:, c], prod, ALU.add)
                    tt_(prod, M, rep(base2, NT), ALU.mult)
                    red(slf[:, c], prod, ALU.add)
                ts_(kk, rr, float(P), None, ALU.is_ge)
                tt_(slf, slf, blk, ALU.subtract)
                tt_(slf, slf, kk, ALU.mult)
                for c in (2, 3):
                    stt(kk, rr, float(c * P), kk, ALU.is_ge, ALU.add)
                    dve.drain()
                tt_(blk, blk, slf, ALU.add)
                tt_(blk, blk, kk, ALU.add)
                stt(rmod, kk, -float(P), rr, ALU.mult, ALU.add)
                dve.drain()
                stt(slf, blk, float(P), rmod, ALU.mult, ALU.add)
                dve.drain()
                dve.tensor_copy(sloti, slf)
                for c in range(2):
                    for tt in range(NT):
                        n = c * NT + tt
                        dve.tensor_scalar(R[n], iota[:], rmod[:, c, tt:tt + 1], None, ALU.is_equal)
                        dve.tensor_scalar(Bm[:, n, :], iota[:, 0:NB], blk[:, c, tt:tt + 1], tokid[:, tt:tt + 1],
                                          ALU.is_equal, ALU.mult)
                dve.drain().then_inc(sem(f"d_r.{l}"), 1)
                dve.wait_ge(sem(f"pe_idx.{l}"), count(f"pe_idx.{l}", 1))
                dve.tensor_copy(idx, bank[6][:, 0:NB]).then_inc(sem(f"d_idx.{l}"), 1)

                def turned(b, par):
                    dve.wait_ge(sem(f"pe_t.{l}"), count(f"pe_t.{l}", b * 2 + 1))
                    if due(b - 1):
                        dve.wait_ge(sem(f"pe_h.{l}"), count(f"pe_h.{l}", b - 1))
                    for k in range(4):
                        dve.tensor_scalar(xgT[par][:, k, :], bank[0][:, k * P:(k + 1) * P], acol[:, i, k:k + 1],
                                          modcol[:, 3 * i, k:k + 1], ALU.mult, ALU.add)
                    dve.drain().then_inc(sem(f"t_ev0.{l}"), 1)

                def hidden(b, par):
                    dve.wait_ge(sem(f"a_mt.{l}"), count(f"a_mt.{l}", b + 1))
                    stt(mh1, mth, 1.0, bank[2 + par][:, 0:FH], ALU.add, ALU.mult)
                    dve.drain()
                    if due(b):
                        dve.wait_ge(sem(f"pe_ht.{l}"), count(f"pe_ht.{l}", b))
                    dve.tensor_tensor(hid, mh1, bank[2 + par][:, FH:2 * FH], ALU.mult).then_inc(sem(f"d_hid.{l}"), 1)

                def result(b, par, n):
                    dve.wait_ge(sem(f"pe_o.{l}"), count(f"pe_o.{l}", b + 1))
                    if due(n * 16):
                        dve.wait_ge(sem(f"y_stored_{par}.{l}"), count(f"y_stored_{par}.{l}", n * 16))
                    dve.tensor_copy(yo[par][:, 512:], bank[7][:]).then_inc(sem(f"d_yo.{l}"), 1)

                turned(0, 0)
                hidden(0, 0)
                turned(1, 1)
                hidden(1, 1)
                turned(2, 0)
                result(0, 0, 0)
                with dve.Fori(1, NB // 2) as ii:
                    hidden(ii * 2, 0)
                    turned(ii * 2 + 1, 1)
                    result(ii * 2 - 1, 1, ii - 1)
                    hidden(ii * 2 + 1, 1)
                    turned(ii * 2 + 2, 0)
                    result(ii * 2, 0, ii)
                hidden(NB - 1, 0)
                result(NB - 2, 1, NB // 2 - 1)
                result(NB - 1, 0, NB // 2)

                for tt in range(NT):
                    dve.wait_ge(sem(f"yg_{tt % 2}.{l}"), count(f"yg_{tt % 2}.{l}", 32 * (tt // 2 + 1)))
                    a, b = yg[tt % 2]
                    ts_(a, a, wc1[:, tt:tt + 1], None, ALU.mult)
                    stt(a, b, wc2[:, tt:tt + 1], a, ALU.mult, ALU.add)
                    dve.drain()
                    dve.tensor_tensor(a, a, gatebc, ALU.mult)
                    dve.drain()
                    dve.tensor_tensor(x[:, tt], x[:, tt], a, ALU.add).then_inc(sem(f"x_up.{2 + 2 * l}"), 1)

            moe(0)

            norm(2)
            gate(2, (2, 3), gatebc1)
            dve.wait_ge(sem("pe_wi"), 1)
            dve.tensor_scalar(wi.rearrange("p t h -> p (t h)"), bank[2][:, 0:NT * IH], IH ** -0.5, None, ALU.mult).then_inc(sem("d_wi"), 1)
            dve.tensor_copy(sel[:, 0, 0:P], causal[:])
            dve.drain()

            def index(tt):
                w = (tt + 1) * P
                s = sel[:, tt, 0:w]
                n = (tt - 1) * IH
                for h in range(IH):
                    dve.wait_ge(sem("a_rel"), n + h + 1)
                    if h == 0:
                        dve.tensor_scalar(s, rel[(n + h) % 2][:, 0:w], wi[:, tt, 0:1], None, ALU.mult).then_inc(sem("d_acc"), 1)
                    else:
                        stt(s, rel[(n + h) % 2][:, 0:w], wi[:, tt, h:h + 1], s, ALU.mult, ALU.add).then_inc(sem("d_acc"), 1)
                    dve.drain()

            def choose(tt):
                w = (tt + 1) * P
                s = sel[:, tt, 0:w]
                tt_(sel[:, tt, tt * P:w], sel[:, tt, tt * P:w], causal[:], ALU.add)
                for _ in range(TOPK // 8):
                    dve.max(out=max8, in_=s)
                    dve.drain()
                    dve.match_replace(out=s, in_to_replace=max8, in_values=s, imm_value=TAKEN)
                    dve.drain()
                dve.tensor_scalar(s, s, TAKEN * 0.5, NEG, ALU.is_gt, ALU.mult)
                dve.drain()

            for tt in range(1, NT):
                index(tt)
            for tt in range(NT):
                b0 = 3 * (tt % 2)
                dve.wait_ge(sem("a_sqs"), tt + 1)
                dve.tensor_reduce(hss, sqs.rearrange("p (h d) -> p h d", d=HD), AX.X, ALU.add).then_inc(sem("d_hss"), 1)
                dve.wait_ge(sem("p_hrs"), tt + 1)
                if due(3 * tt):
                    dve.wait_ge(sem("pe_qk"), 3 * tt)
                for i in range(2):
                    dve.tensor_tensor(heads(qkn[:, i * 512:(i + 1) * 512]), heads(bank[b0 + i][:]),
                                      bc(hrs[:, 8 * i:8 * i + 8], HD), ALU.mult)
                for i in range(2):
                    dve.tensor_tensor(qkn[:, D:].rearrange("p (h r d) -> p r h d", r=2, d=HD)[:, i],
                                      heads(bank[b0 + 2][:, 0:KVH * HD]), bc(hrs[:, QH:], HD), ALU.mult)
                dve.drain().then_inc(sem("d_qkn"), 1)
                if tt < NT - 1:
                    choose(tt + 1)
            for u in range(16):
                tt, kv = u // 4, u % 4
                w = (tt + 1) * P
                for i in range(4):
                    dve.wait_ge(sem("pe_s"), 4 * u + i + 1)
                    if i == 0:
                        if due(chunks_before(u - 1)):
                            dve.wait_ge(sem("pe_pt"), chunks_before(u - 1))
                    dve.tensor_tensor_reduce(out=Sm[u % 2][:, i, 0:w], in0=bank[i][:, 0:w], in1=sel[:, tt, 0:w],
                                             scale=HD ** -0.5, scalar=-3e38, op0=ALU.add, op1=ALU.max,
                                             accum_out=nmx[:, kv, i:i + 1]).then_inc(sem("d_sm"), 1)
                dve.drain()
                dve.tensor_scalar(nmx[:, kv], nmx[:, kv], -1.0, None, ALU.mult).then_inc(sem("d_nmx"), 1)
                if kv == 3:
                    dve.wait_ge(sem("a_exp"), 4 * u + 4)
                    dve.reciprocal(rinv, rsum)
                    dve.drain()
                    dve.wait_ge(sem("pe_pv"), u + 1)
                    for hh in range(2):
                        dve.tensor_tensor(heads(o[:, hh * 512:(hh + 1) * 512]), heads(bank[6 + hh][:]),
                                          bc(rinv[:, 8 * hh:8 * hh + 8], HD), ALU.mult)
                    dve.drain().then_inc(sem("d_o"), 1)
                    for hh in range(2):
                        half = slice(hh * 512, (hh + 1) * 512)
                        dve.wait_ge(sem("pe_xo"), 2 * tt + hh + 1)
                        dve.tensor_tensor(o[:, half], bank[6 + hh][:], gatebc1[:, half], ALU.mult).then_inc(sem("d_xo"), 1)
                    dve.drain()
                    dve.tensor_tensor(x[:, tt], x[:, tt], o, ALU.add).then_inc(sem("x_up.3"), 1)
                    dve.drain()
            moe(1)


INPUTS = ["x", "c", "ada_w", "ada_b", "norm_mix", "norm_ffn", "ssd_w_in", "ssd_conv_w", "ssd_conv_b", "ssd_dt_bias",
          "ssd_a_log", "ssd_d", "ssd_norm", "ssd_w_out", "dsa_w_in", "dsa_q_norm", "dsa_k_norm", "dsa_w_out",
          "moe_w_group", "moe_b_group", "moe_w_expert", "moe_b_expert", "moe_w1", "moe_w3", "moe_w2"]


def kernel(**inputs):
    import concourse.bacc as bacc
    from concourse.bass_utils import run_bass_kernel_spmd

    nc = bacc.Bacc("TRN2", target_bir_lowering=False, num_devices=1)
    arrays, tensors = {}, {}
    for name in INPUTS:
        a = np.ascontiguousarray(inputs[name])
        arrays["in_" + name] = a
        tensors[name] = nc.dram_tensor("in_" + name, a.shape, mybir.dt.from_np(a.dtype), kind="ExternalInput").ap()
    tensors["out"] = nc.dram_tensor("out", (1, SEQ, D), F32, kind="ExternalOutput").ap()
    build(nc, tensors)
    result = run_bass_kernel_spmd(nc, [arrays], core_ids=[0])
    return result.results[0]["out"]
```

```python
from contextlib import ExitStack

import numpy as np

import concourse.bass as bass
from concourse import mybir

F32 = mybir.dt.float32
I32 = mybir.dt.int32
ALU = mybir.AluOpType
ACT = mybir.ActivationFunctionType
AX = mybir.AxisListType

P = 128
D = 1024
SEQ = 512
NT = SEQ // P
KD = D // P
EPS = 1e-6
NEG = -1e30
TAKEN = -3e38

DI = 2048
G = 8
HEADS = 32
HD = 64
NS = 128
GC = DI // G
JH = HEADS // G
OFF_Z, OFF_X, OFF_B, OFF_C, OFF_DT = 0, DI, 2 * DI, 2 * DI + G * NS, 2 * DI + 2 * G * NS
CT = DI // P
CONV_TILES = (DI + 2 * G * NS) // P
GW = 2 * GC + 2 * NS
LOG1P_TERMS = 8

QH, KVH = 16, 4
IH = 8
TOPK = min(256, SEQ // 4)
QK_HEADS = QH + KVH
OFF_Q, OFF_K, OFF_V = 0, 1024, 1280
OFF_QI, OFF_KI, OFF_WI = 1536, 2048, 2112

NG, EG = 4, 4
NE = NG * EG
FH = 256
OVER = 2 * SEQ // (P + 1)
NB = NE + OVER

ADA_SLOT = KD * D
EXPERT_SLOT = KD * 2 * FH + 2 * D


PER_USE = {
    "n_sq": NT, "n_rs": 1, "n_xn": NT, "n_col": 1, "n_tr": KD, "n_ev0": KD // 2, "n_ev1": KD // 2,
    "pe_gate": 2, "d_gate": 2, "x_up": NT,
    "xn_stored": 16, "rt_in": 64, "pe_rt": 1, "d_g": 1, "d_e": 1, "a_r": 2, "d_m": 1, "pe_rank": 1, "d_r": 1,
    "pe_idx": 1, "d_idx": 1, "over_ids": 1,
    "exp13_0": 32 * ((NB + 1) // 2), "exp13_1": 32 * (NB // 2), "exp2_0": 16 * ((NB + 1) // 2), "exp2_1": 16 * (NB // 2),
    "y_stored_0": 16 * ((NB + 1) // 2), "y_stored_1": 16 * (NB // 2),
    "pe_t": 2 * NB, "t_ev0": NB, "t_ev1": NB, "pe_h": NB, "a_mt": NB, "d_hid": NB, "pe_ht": NB, "a_ht": NB, "pe_o": NB,
    "d_yo": NB, "yg_0": 32, "yg_1": 32, "yg_2": 32, "yg_3": 32,
}
CREDIT = ("pe_df", "pe_st", "pe_yt", "d_bt", "a_ex", "a_yn", "a_ye", "d_skip", "d_cb", "d_w", "d_y", "d_st", "d_mu",
          "d_ad", "p_y")


def build(nc, t):
    with ExitStack() as ctx:
        def sb(name, shape, dt=F32):
            return ctx.enter_context(nc.sbuf_tensor(name, shape, dt))

        sems = {}

        def sem(name):
            name = name.split(".")[0]
            if name not in sems:
                sems[name] = ctx.enter_context(nc.semaphore(name))
            return sems[name]

        def count(name, value):
            base, _, use = name.partition(".")
            if use:
                value = value + (int(use) - (base == "x_up")) * PER_USE[base]
            return value + (base in CREDIT)

        def due(value):
            return not isinstance(value, int) or value > 0

        def chunks_before(u):
            tt, kv = max(u, 0) // 4, max(u, 0) % 4
            return 4 * (tt * (tt + 1) // 2) + kv * (tt + 1)

        def credit(eng, names):
            for name in names:
                eng.sem_inc(sem(name), 1)

        bank = [ctx.enter_context(nc.psum_tensor(f"bank{i}", [P, 512], F32)) for i in range(8)]
        xn_dram = [nc.dram_tensor(f"xn_rows{l}", (SEQ, D), F32, kind="Internal").ap() for l in range(2)]
        y_dram = nc.dram_tensor("slot_rows", (NB * P, D), F32, kind="Internal").ap()

        x = sb("x_res", [P, NT, D])
        xn = sb("xn", [P, NT, D])
        hT = sb("hT", [P, KD, SEQ])
        wts = sb("wts", [P, 2 * EXPERT_SLOT + ADA_SLOT])
        ident = sb("ident", [P, P])
        upto = sb("upto", [P, P])
        after = sb("after", [P, P])
        before = sb("before", [P, P])
        causal = sb("causal", [P, P])
        ones = sb("ones", [P, P])
        iota = sb("iota", [P, P])
        tokid = sb("tokid", [P, NT])
        pref = sb("pref", [P, NT, 4])
        ccol = sb("ccol", [P, KD])
        cond = sb("cond", [P, KD])
        modcol = sb("modcol", [P, 12, KD])
        adab = sb("adab", [P, 12, KD])
        normw = sb("normw", [P, 4, KD])
        acol = sb("acol", [P, 4, KD])
        ssq = sb("ssq", [P, 4, NT])
        rstd = sb("rstd", [P, 4, NT])
        expo = sb("expo", [P, QK_HEADS])

        epst = sb("epst", [P, 1])
        work = sb("work", [P, 18944])

        class Carve:
            def __init__(self):
                self.at = 0

            def __call__(self, *shape, dt=F32):
                n = int(np.prod(shape))
                v = work[:, self.at:self.at + n]
                self.at += n
                assert self.at <= 18944, self.at
                if dt is not F32:
                    v = v.bitcast(dt)
                if len(shape) == 2:
                    v = v.rearrange("p (a b) -> p a b", b=shape[1])
                if len(shape) == 3:
                    v = v.rearrange("p (a b c) -> p a b c", b=shape[1], c=shape[2])
                return v

        xn_flat = xn[:].rearrange("p t d -> p (t d)")
        slot = [wts[:, i * EXPERT_SLOT:(i + 1) * EXPERT_SLOT] for i in range(2)]
        ada_buf = wts[:, 2 * EXPERT_SLOT:]

        cv = Carve()
        yT = cv(CT, SEQ)
        zs = [cv(NT, GC) for _ in range(2)]
        upad_at = cv.at
        upad = [cv(516) for _ in range(2)]
        cacc = [cv(SEQ) for _ in range(2)]
        th = [cv(SEQ) for _ in range(2)]
        xdt, skip, xd, yb, yn, zt, state = (cv(GC) for _ in range(7))
        decay, wmat = cv(JH, P), cv(JH, P)
        btok, cbm = cv(P), cv(P)
        tria = [cv(JH, P) for _ in range(2)]
        dtw = xd.rearrange("p (k h) -> p k h", h=HEADS)
        s1, s2 = (v.rearrange("p (t h) -> p t h", h=HEADS) for v in (btok, cbm))
        dt, aa, acs, ea, dte, s3 = (cv(NT, HEADS) for _ in range(6))
        dtb, alog, dsk = cv(HEADS), cv(HEADS), cv(HEADS)
        prow, brow = th[0][:, 0:P], th[1][:, 0:P]
        cwT = cv(5, CONV_TILES)
        nwT = cv(CT)
        gp = [cv(4, 5) for _ in range(2)]
        gn_w = [cv(2) for _ in range(2)]
        yss, yrs = cv(1), cv(1)
        gatebc0 = zs[0].rearrange("p a b -> p (a b)")
        xbcT = [xn_flat[:, i * 2048:(i + 1) * 2048].rearrange("p (a b) -> p a b", b=SEQ) for i in range(2)]

        mv = Carve()
        xg = [mv(D) for _ in range(2)]
        xgT = [mv(KD, P) for _ in range(2)]
        mth, mh1, hid = mv(FH), mv(FH), mv(FH)
        hidT = mv(2, P)
        yo = [mv(D) for _ in range(2)]
        yg = [[mv(D) for _ in range(2)] for _ in range(2)] + [xg, [v.rearrange("p k t -> p (k t)") for v in xgT]]
        gatebc = mv(D)
        rtw = mv(KD, NG + NE)
        rtb = mv(NG + NE)
        lg = mv(NT, NG + NE)
        gsh, cand, goh, ein, oh1, oh2, m4 = (mv(NT, 4) for _ in range(7))
        prod = mv(NT, NE)
        picked = [mv(2, NT, NE) for _ in range(3)]
        M = mv(2, NT, NE)
        MM, rank, toff = (mv(NT, NE) for _ in range(3))
        g1, g2, g3, wc1, wc2, mx1, mx2 = (mv(NT) for _ in range(7))
        tot, over, cumi, base2 = (mv(NE) for _ in range(4))
        rr, kk, rmod, blk, slf = (mv(2, NT) for _ in range(5))
        sloti = mv(2, NT, dt=I32)
        R = [mv(P) for _ in range(8)]
        Bm = mv(8, NB)
        idx = mv(NB, dt=I32)
        ovt = mv(OVER, NE)
        ovf = mv(OVER)
        ovi = mv(OVER + 1, dt=I32)

        av = Carve()
        qkn = av(QH * HD + 2 * KVH * HD)
        V = av(NT, KVH * HD)
        qT = av(8, SEQ)
        kT = av(KVH, SEQ)
        qiT = av(4, SEQ)
        kiT = av(SEQ)
        sel = av(NT, SEQ)
        PT = av(4, 4 * P)
        o = av(D)
        oT = av(KD, P)
        kiw = o.rearrange("p (k n) -> p k n", k=KD)
        rel = [oT[:, 4 * i:4 * i + 4, :].rearrange("p a b -> p (a b)") for i in range(2)]
        wiw = av(KD, IH)
        wi = av(NT, IH)
        hss, hrs = av(QK_HEADS), av(QK_HEADS)
        qkw = av(2)
        max8 = av(8)
        nmx, rinv = av(4, 4), av(QH)
        rsum = av(2, QH)
        gatebc1 = av(D)
        Sm = [xn_flat[:, i * 2048:(i + 1) * 2048].rearrange("p (a b) -> p a b", b=SEQ) for i in range(2)]
        sqs = xn_flat[:, 0:QK_HEADS * HD]

        w13 = [s[:, 0:KD * 2 * FH].rearrange("p (k f) -> p k f", k=KD) for s in slot]
        w2s = [s[:, KD * 2 * FH:].rearrange("p (k n) -> p k n", k=2) for s in slot]
        gw = [s.rearrange("p (k f) -> p k f", k=KD) for s in slot]
        wo_ssd = [wts[:, i * 4096:(i + 1) * 4096].rearrange("p (c n) -> p c n", c=4) for i in range(3)]
        ada = [ada_buf.rearrange("p (k n) -> p k n", k=KD), yT.rearrange("p c t -> p (c t)").rearrange("p (k n) -> p k n", k=KD)]
        late_sum = [zs[1].rearrange("p a b -> p (a b)"), work[:, upad_at:upad_at + D]]
        wq = [ada_buf[:, i * 4096:(i + 1) * 4096].rearrange("p (k f) -> p k f", k=KD) for i in range(2)]
        wkv = wts[:, 0:4096].rearrange("p (k f) -> p k f", k=KD)
        wqi = wts[:, 4096:8192].rearrange("p (k f) -> p k f", k=KD)
        wo_dsa = ada_buf.rearrange("p (c n) -> p c n", c=KD)

        w_in = t["ssd_w_in"][0].rearrange("(p k) n -> p k n", k=KD)
        ada_d = t["ada_w"].rearrange("l (p k) (j n) -> l j p k n", k=KD, j=6)
        dsa_in = t["dsa_w_in"][0].rearrange("(p k) n -> p k n", k=KD)

        def bc(ap, n):
            return ap.unsqueeze(2).broadcast_to([ap.shape[0], ap.shape[1], n])

        def rep(ap, n):
            return ap.unsqueeze(1).broadcast_to([ap.shape[0], n, ap.shape[1]])

        def row_bc(ap, n):
            return ap.rearrange("(o n) -> o n", o=1).broadcast_to([P, n])

        def overflow(eng, l):
            eng.wait_ge(sem(f"over_ids.{l}"), count(f"over_ids.{l}", 1))
            return eng.value_load(ovi[0:1, OVER:OVER + 1], min_val=0, max_val=OVER)

        def filled(eng, n, filling, b):
            return eng.If(b - NE < filling + n if n > 0 else b - n - NE < filling)

        def top_up(eng, filling, per_block):
            for b in range(NE, NB):
                with eng.If(filling < b - NE + 1):
                    for name, n in per_block:
                        eng.sem_inc(sem(name.format(par=b % 2)), n)

        block = ctx.enter_context(nc.Block())

        @block.sync
        def _(sp):
            def load_ada(i, buf, s):
                sp.dma_start(buf, ada_d[i // 6, i % 6]).then_inc(s, 16)

            def load_group(g, par):
                s = sem(f"group_w{par}")
                for dst, col, n in ((0, OFF_X, GC), (GC, OFF_B, NS), (GC + NS, OFF_C, NS), (GC + 2 * NS, OFF_Z, GC)):
                    sp.dma_start(gw[par][:, :, dst:dst + n], w_in[:, :, bass.DynSlice(g * n + col, n)]).then_inc(s, 16)

            sp.dma_start(x[:], t["x"][0].rearrange("(t p) d -> p t d", p=P)).then_inc(sem("x_in"), 16)
            for n in range(2):
                for q in range(4):
                    sp.dma_start(ada[n][:, 2 * q:2 * q + 2], ada_d[0, n][:, 2 * q:2 * q + 2]).then_inc(sem(f"ada_first{n}{q}"), 16)
            load_group(0, 0)
            load_group(1, 1)
            sp.wait_ge(sem("pe_ada"), 1)
            load_ada(2, ada[0], sem("ada_in"))

            def ssd_loads(g, par, last):
                if not last:
                    sp.wait_ge(sem("pe_z"), g * NT + NT)
                    load_group(g + 2, par)
                sp.wait_ge(sem("pe_ad"), g + 1)
                load_ada(g + 3, ada[0], sem("ada_in"))
            for g in range(G):
                ssd_loads(g, g % 2, g >= G - 2)
                if g == 0:
                    for n in range(0, OVER * P, SEQ):
                        rows = min(SEQ, OVER * P - n)
                        sp.dma_start(y_dram[NE * P + n:NE * P + n + rows, :], t["x"][0, 0:rows, :]).then_inc(sem("rows_set"), 16)
            for c in range(3):
                if c == 0:
                    sp.wait_ge(sem("pe_z"), NT * G)
                sp.dma_start(wo_ssd[c], t["ssd_w_out"][0, c * 512:(c + 1) * 512, :].rearrange("(c p) n -> p c n", p=P)
                             ).then_inc(sem(f"wo_in{c}"), 16)
            sp.wait_ge(sem("pe_wo"), 1)
            sp.dma_start(wo_ssd[0], t["ssd_w_out"][0, 1536:2048, :].rearrange("(c p) n -> p c n", p=P)
                         ).then_inc(sem("wo_in0"), 16)
            sp.wait_ge(sem("d_late"), 1)
            load_ada(11, ada[0], sem("ada_in"))

            def load_expert(l, e, par):
                s = sem(f"exp13_{par}.{l}")
                for i, w in enumerate(("moe_w1", "moe_w3")):
                    src = t[w][l].rearrange("e (p k) f -> e p k f", k=KD)[bass.DynSlice(e, 1)].rearrange("o p k f -> (o p) k f")
                    sp.dma_start(w13[par][:, :, i * FH:(i + 1) * FH], src).then_inc(s, 16)

            def load_w2(l, e, par):
                src = t["moe_w2"][l].rearrange("e (p k) n -> e p k n", k=2)[bass.DynSlice(e, 1)].rearrange("o p k n -> (o p) k n")
                sp.dma_start(w2s[par], src).then_inc(sem(f"exp2_{par}.{l}"), 16)

            def moe_loads(l):
                load_expert(l, 0, 0)
                load_w2(l, 0, 0)
                load_expert(l, 1, 1)
                load_w2(l, 1, 1)
                with sp.Fori(0, NE // 2 - 1) as i:
                    for par in range(2):
                        sp.wait_ge(sem(f"pe_h.{l}"), count(f"pe_h.{l}", i * 2 + par + 1))
                        load_expert(l, i * 2 + par + 2, par)
                        sp.wait_ge(sem(f"pe_o.{l}"), count(f"pe_o.{l}", i * 2 + par + 1))
                        load_w2(l, i * 2 + par + 2, par)
                filling = overflow(sp, l)
                with sp.Fori(NE // 2, (NB + 1) // 2) as i:
                    for par in range(2):
                        with filled(sp, 0, filling, i * 2 + par):
                            e = sp.value_load(ovi[0:1, bass.DynSlice(i * 2 + par - NE, 1)], min_val=0, max_val=NE - 1)
                            sp.wait_ge(sem(f"pe_h.{l}"), count(f"pe_h.{l}", i * 2 + par - 1))
                            load_expert(l, e, par)
                            sp.wait_ge(sem(f"pe_o.{l}"), count(f"pe_o.{l}", i * 2 + par - 1))
                            load_w2(l, e, par)
                return filling

            sp.wait_ge(sem("pe_wo"), 3 + NT)
            filling = moe_loads(0)
            sp.wait_ge(sem("d_late"), 2)
            for i in range(2):
                sp.dma_start(wq[i], dsa_in[:, :, OFF_Q + i * 512:OFF_Q + (i + 1) * 512]).then_inc(sem("wq_in"), 16)
            sp.wait_ge(sem("x_up.2"), count("x_up.2", NT))
            top_up(sp, filling, (("exp13_{par}", 32), ("exp2_{par}", 16)))
            sp.dma_start(wqi, dsa_in[:, :, OFF_QI:OFF_QI + 512]).then_inc(sem("wqi_in"), 16)
            for i in range(2):
                sp.dma_start(kiw[:, :, i * HD:(i + 1) * HD], dsa_in[:, :, OFF_KI:OFF_KI + HD]).then_inc(sem("wqi_in"), 16)
                sp.dma_start(qkw[i * HD:(i + 1) * HD, 0:1], t["dsa_q_norm"].rearrange("o (d a) -> d (o a)", a=1)).then_inc(sem("wqi_in"), 16)
                sp.dma_start(qkw[i * HD:(i + 1) * HD, 1:2], t["dsa_k_norm"].rearrange("o (d a) -> d (o a)", a=1)).then_inc(sem("wqi_in"), 16)
            sp.dma_start(wiw, dsa_in[:, :, OFF_WI:OFF_WI + IH]).then_inc(sem("wqi_in"), 16)
            sp.dma_start(wkv, dsa_in[:, :, OFF_K:OFF_K + 512]).then_inc(sem("wkv_in"), 16)
            sp.wait_ge(sem("pe_qkv"), NT)
            sp.dma_start(wo_dsa, t["dsa_w_out"][0].rearrange("(c p) n -> p c n", p=P)).then_inc(sem("wo_dsa_in"), 16)
            moe_loads(1)
            for i in range(NT):
                sp.wait_ge(sem("x_up.4"), count("x_up.4", i + 1))
                sp.dma_start(t["out"][0, i * P:(i + 1) * P, :], x[:, i, :]).then_inc(sem("out_stored"), 16)
            sp.wait_ge(sem("out_stored"), 16 * NT)

        @block.gpsimd
        def _(pool):
            credit(pool, [n for n in CREDIT if n[0] == "p" and n[1] == "_"])
            def mask(tile, inside, fill, op, step):
                pool.memset(tile[:], inside)
                pool.drain()
                pool.affine_select(out=tile[:], in_=tile[:], compare_op=op, fill=fill, base=0,
                                   pattern=[[-step, P]], channel_multiplier=step)
            mask(ident, 0.0, 1.0, ALU.not_equal, 1)
            mask(upto, 1.0, 0.0, ALU.is_ge, -1)
            mask(after, 1.0, 0.0, ALU.is_gt, 1)
            mask(before, 1.0, 0.0, ALU.is_gt, -1)
            mask(causal, 0.0, NEG, ALU.is_ge, 1)
            pool.memset(ones[:], 1.0)
            pool.iota(iota[:], pattern=[[1, P]], base=0, channel_multiplier=0, allow_small_or_imprecise_dtypes=True)
            pool.iota(tokid[:], pattern=[[P, NT]], base=0, channel_multiplier=1, allow_small_or_imprecise_dtypes=True)
            pool.iota(pref[:], pattern=[[0, NT], [-1, 4]], base=4, channel_multiplier=0, allow_small_or_imprecise_dtypes=True)
            pool.memset(expo[:], -0.5)
            pool.memset(epst[:], EPS)
            for i in range(2):
                pool.memset(upad[i][:, 0:3], 0.0)
            pool.drain().then_inc(sem("consts"), 1)

            def norm(i):
                pool.wait_ge(sem(f"n_sq.{i}"), count(f"n_sq.{i}", NT))
                pool.tensor_scalar(rstd[:, i], ssq[:, i], 1.0 / D, EPS, ALU.mult, ALU.add)
                pool.drain()
                pool.tensor_tensor(rstd[:, i], rstd[:, i], expo[:, 0:NT], ALU.pow).then_inc(sem(f"n_rs.{i}"), 1)

            norm(0)

            def params(gn, par):
                pool.tensor_copy(gp[par][:, 0:2, :], cwT[:, :, bass.DynSlice(gn * 2, 2)].rearrange("p a c -> p c a"))
                pool.tensor_copy(gp[par][:, 2:3, :], cwT[:, :, bass.DynSlice(gn + CT, 1)].rearrange("p a c -> p c a"))
                pool.tensor_copy(gp[par][:, 3:4, :], cwT[:, :, bass.DynSlice(gn + CT + G, 1)].rearrange("p a c -> p c a"))
                pool.tensor_copy(gn_w[par], nwT[:, bass.DynSlice(gn * 2, 2)])
                pool.drain().then_inc(sem("p_gp"), 1)

            def triangle(g, j, m):
                if due(m - 1):
                    pool.wait_ge(sem("pe_df"), count("pe_df", m - 1))
                pool.tensor_tensor(tria[j % 2], rep(upto[:], JH), bc(aa[:, j, bass.DynSlice(g * JH, JH)], P),
                                   ALU.mult).then_inc(sem("p_tri"), 1)

            pool.wait_ge(sem("d_par"), 1)
            params(0, 0)
            pool.wait_ge(sem("d_dt"), 1)
            triangle(0, 0, 0)

            def step(g, j, par, last):
                m = g * NT + j
                if not (last and j == NT - 1):
                    if j < NT - 1:
                        triangle(g, j + 1, m + 1)
                    else:
                        triangle(g + 1, 0, m + 1)
                if j < NT - 1:
                    pool.wait_ge(sem("d_xdt"), m + 1)
                    if due(g * (NT - 1) + j):
                        pool.wait_ge(sem("pe_st"), count("pe_st", g * (NT - 1) + j))
                    pool.tensor_tensor(xd.rearrange("p (h d) -> p h d", d=HD), xdt.rearrange("p (h d) -> p h d", d=HD),
                                       bc(dte[:, j, bass.DynSlice(g * JH, JH)], HD), ALU.mult).then_inc(sem("p_xd"), 1)
                pool.wait_ge(sem("d_y"), count("d_y", m + 1))
                pool.wait_ge(sem("d_zs"), m + 1)
                pool.tensor_tensor(yb, yb, skip, ALU.add)
                pool.drain()
                pool.tensor_tensor(yb, yb, zs[par][:, j], ALU.mult).then_inc(sem("p_y"), 1)
                pool.wait_ge(sem("a_sq"), m + 1)
                pool.tensor_tensor(yrs, yss, epst[:], ALU.add)
                pool.drain()
                pool.tensor_tensor(yrs, yrs, expo[:, 0:1], ALU.pow).then_inc(sem("p_rs"), 1)

            def group(g, par, last):
                if not last:
                    if due(g * NT):
                        pool.wait_ge(sem("a_ye"), count("a_ye", g * NT))
                    if due(g * NT):
                        pool.wait_ge(sem("d_mu"), count("d_mu", g * NT))
                    params(g + 1, 1 - par)
                for j in range(NT):
                    step(g, j, par, last)

            with pool.Fori(0, G // 2 - 1) as i:
                group(i * 2, 0, False)
                group(i * 2 + 1, 1, False)
            group(G - 2, 0, False)
            group(G - 1, 1, True)

            def moe(l):
                norm(1 + 2 * l)
                pool.wait_ge(sem(f"xn_stored.{l}"), count(f"xn_stored.{l}", 16))
                pool.wait_ge(sem(f"d_idx.{l}"), count(f"d_idx.{l}", 1))
                filling = overflow(pool, l)

                def gather(b):
                    if due(2 * (b - 1)):
                        pool.wait_ge(sem(f"pe_t.{l}"), count(f"pe_t.{l}", 2 * (b - 1)))
                    pool.indirect_dma_start(xg[b % 2], None, xn_dram[l],
                                            bass.IndirectOffsetOnAxis(ap=idx[:, b:b + 1], axis=0)).then_inc(sem(f"gath{l}_{b % 2}"), 16)
                for b in range(NE):
                    gather(b)
                for b in range(NE, NB):
                    with pool.If(filling > b - NE):
                        gather(b)
                for i in range(2):
                    pool.wait_ge(sem(f"y_stored_{i}.{l}"), count(f"y_stored_{i}.{l}", 16 * (NE // 2)))
                for b in range(NE, NB):
                    with pool.If(filling > b - NE):
                        pool.wait_ge(sem(f"y_stored_{b % 2}.{l}"), count(f"y_stored_{b % 2}.{l}", 16 * (b // 2 + 1)))
                for tt in range(NT):
                    for c in range(2):
                        pool.indirect_dma_start(yg[tt][c], None, y_dram,
                                                bass.IndirectOffsetOnAxis(ap=sloti[:, c, tt:tt + 1], axis=0)
                                                ).then_inc(sem(f"yg_{tt}.{l}"), 16)
                return filling

            moe(0)
            norm(2)
            for tt in range(NT):
                pool.wait_ge(sem("d_hss"), tt + 1)
                pool.tensor_scalar(hrs, hss, 1.0 / HD, EPS, ALU.mult, ALU.add)
                pool.drain()
                pool.tensor_tensor(hrs, hrs, expo[:], ALU.pow).then_inc(sem("p_hrs"), 1)
            moe(1)

        @block.tensor
        def _(pe):
            credit(pe, [n for n in CREDIT if n[:2] == "pe"])
            def mm(out, lhsT, rhs, k, n):
                return pe.matmul(out, lhsT, rhs, start=(k == 0), stop=(k == n - 1))

            def ada_columns(rows, at=0):
                for k in range(KD):
                    last = pe.matmul(bank[7][:, GC + at + k:GC + at + k + 1], rows[:, k:D:KD], ones[:, 0:1], start=True, stop=True)
                return last

            def norm(i):
                pe.wait_ge(sem(f"n_xn.{i}"), count(f"n_xn.{i}", NT))
                for k in range(KD):
                    if k >= 2:
                        pe.wait_ge(sem(f"n_ev{k % 2}.{i}"), count(f"n_ev{k % 2}.{i}", k // 2))
                    for tt in range(NT):
                        last = pe.transpose(bank[k % 2][:, tt * P:(tt + 1) * P], xn[:, tt, k:D:KD], ident[:])
                    last.then_inc(sem(f"n_tr.{i}"), 1)

            def hT_ready(i):
                pe.wait_ge(sem(f"n_ev0.{i}"), count(f"n_ev0.{i}", KD // 2))
                pe.wait_ge(sem(f"n_ev1.{i}"), count(f"n_ev1.{i}", KD // 2))

            def gate(i, banks):
                for k in range(KD):
                    last = pe.matmul(bank[banks[k // 4]][:, (k % 4) * P:(k % 4 + 1) * P],
                                     modcol[:, 3 * i + 2, k:k + 1].broadcast_to([P, P]), ident[:], start=True, stop=True)
                    if k % 4 == 3:
                        last.then_inc(sem(f"pe_gate.{i}"), 1)

            pe.wait_ge(sem("consts"), 1)
            pe.wait_ge(sem("par_in"), 160)
            pe.transpose(bank[2][:, 0:P], prow, ident[:])
            pe.transpose(bank[2][:, P:P + CONV_TILES + CT], brow[0:CONV_TILES + CT, :],
                         ident[0:CONV_TILES + CT, 0:CONV_TILES + CT]).then_inc(sem("pe_par"), 1)
            pe.wait_ge(sem("d_first"), 1)
            ada_columns(ada[0][:, 0]).then_inc(sem("pe_ada"), 1)
            pe.wait_ge(sem("d_first"), 2)
            pe.wait_ge(sem("d_ada"), 1)
            ada_columns(ada[1][:, 0]).then_inc(sem("pe_ada"), 1)
            norm(0)
            hT_ready(0)
            for tt in range(NT):
                for k in range(KD):
                    last = mm(bank[3][:, tt * HEADS:(tt + 1) * HEADS], hT[:, k, tt * P:(tt + 1) * P], dtw[:, k], k, KD)
            last.then_inc(sem("pe_dt"), 1)

            def project_x(gn, par, j):
                n = gn * NT + j
                if due(n - 1):
                    pe.wait_ge(sem("a_xe"), n - 1)
                for k in range(KD):
                    last = mm(bank[j % 2][:], gw[par][:, k, j * P:(j + 1) * P], hT[:, k, :], k, KD)
                last.then_inc(sem("pe_x"), 1)

            def project_z(gn, par, j):
                n = gn * NT + j
                if due(n):
                    pe.wait_ge(sem("d_zs"), n)
                for k in range(KD):
                    last = mm(bank[2][:, 0:GC], hT[:, k, j * P:(j + 1) * P],
                              gw[par][:, k, 2 * GC:], k, KD)
                last.then_inc(sem("pe_z"), 1)

            def scan_in(g, par, j):
                m = g * NT + j
                if j == 0:
                    pe.wait_ge(sem("d_mu"), count("d_mu", g * NT + NT))
                    if due(g):
                        pe.wait_ge(sem("d_ad"), count("d_ad", g))
                cols = slice(j * P, (j + 1) * P)
                if due(m):
                    pe.wait_ge(sem("d_skip"), count("d_skip", m))
                if due(g * (NT - 1) + j):
                    pe.wait_ge(sem("d_bt"), count("d_bt", g * (NT - 1) + j))
                for i in range(3 if j < NT - 1 else 2):
                    last = pe.transpose(bank[3][:, i * P:(i + 1) * P], xbcT[par][:, i, cols], ident[:])
                last.then_inc(sem("pe_xt"), 1)
                if due(m):
                    pe.wait_ge(sem("d_cb"), count("d_cb", m))
                pe.matmul(bank[5][:, 0:P], xbcT[par][:, 2, cols], xbcT[par][:, 3, cols], start=True, stop=True
                          ).then_inc(sem("pe_cb"), 1)
                pe.wait_ge(sem("p_tri"), m + 1)
                if due(m):
                    pe.wait_ge(sem("a_ex"), count("a_ex", m))
                turned_ys = m if j == 0 else m - 1
                if due(turned_ys):
                    pe.wait_ge(sem("a_ye"), count("a_ye", turned_ys))
                pe.matmul(bank[4][:], after[:], tria[j % 2].rearrange("p h l -> p (h l)"), start=True, stop=True
                          ).then_inc(sem("pe_df"), 1)

            def scan_out(g, par, j):
                m = g * NT + j
                if due(m):
                    pe.wait_ge(sem("d_y"), count("d_y", m))
                if j > 0:
                    if due(g * (NT - 1) + j):
                        pe.wait_ge(sem("d_st"), count("d_st", g * (NT - 1) + j))
                    pe.matmul(bank[6][:, GC:2 * GC], xbcT[par][:, 3, j * P:(j + 1) * P], state, start=True, stop=True)
                pe.wait_ge(sem("d_w"), count("d_w", m + 1))
                for h in range(JH):
                    last = pe.matmul(bank[6][:, h * HD:(h + 1) * HD], wmat[:, h, :], xdt[:, h * HD:(h + 1) * HD],
                                     start=True, stop=True)
                last.then_inc(sem("pe_y"), 1)
                if j < NT - 1:
                    pe.wait_ge(sem("p_xd"), g * (NT - 1) + j + 1)
                    pe.wait_ge(sem("d_bt"), count("d_bt", g * (NT - 1) + j + 1))
                    if due(g * (NT - 1) + j):
                        pe.wait_ge(sem("d_st"), count("d_st", g * (NT - 1) + j))
                    pe.matmul(bank[7][:, 0:GC], btok, xd, start=True, stop=True).then_inc(sem("pe_st"), 1)

            def turn_y(g, j):
                m = g * NT + j
                pe.wait_ge(sem("a_yn"), count("a_yn", m + 1))
                pe.wait_ge(sem("a_ex"), count("a_ex", m + (2 if j < NT - 1 else 1)))
                for i in range(2):
                    last = pe.transpose(bank[4][:, i * P:(i + 1) * P], yn[:, i * P:(i + 1) * P], ident[:])
                last.then_inc(sem("pe_yt"), 1)

            pe.wait_ge(sem("group_w0"), 64)
            pe.wait_ge(sem("d_par"), 1)
            project_x(0, 0, 0)
            project_x(0, 0, 1)
            project_z(0, 0, 0)
            pe.wait_ge(sem("d_a"), 1)
            pe.matmul(bank[4][:, 0:P], upto[:], aa.rearrange("p c h -> p (c h)"), start=True, stop=True)
            pe.matmul(bank[4][:, P:2 * P], ones[:], aa.rearrange("p c h -> p (c h)"), start=True, stop=True
                      ).then_inc(sem("pe_cs"), 1)
            project_z(0, 0, 1)
            for j in range(2, NT):
                project_x(0, 0, j)
                project_z(0, 0, j)
            pe.wait_ge(sem("d_dt"), 1)

            def group(g, par, last, even):
                for j in range(NT):
                    scan_in(g, par, j)
                    if not last:
                        if j == 0:
                            pe.wait_ge(sem(f"group_w{1 - par}"), even * 64 + (64 if par == 0 else 128))
                        project_x(g + 1, 1 - par, j)
                    elif j == 0:
                        gate(0, (0, 1))
                    if j > 0:
                        turn_y(g, j - 1)
                    scan_out(g, par, j)
                    if not last:
                        project_z(g + 1, 1 - par, j)
                pe.wait_ge(sem("d_ps"), g + 1)
                ada_columns(ada[0][:, 0]).then_inc(sem("pe_ad"), 1)
                turn_y(g, NT - 1)

            pe.wait_ge(sem("d_ada"), 2)
            with pe.Fori(0, G // 2 - 1) as i:
                group(i * 2, 0, False, i)
                group(i * 2 + 1, 1, False, i)
            group(G - 2, 0, False, G // 2 - 1)
            group(G - 1, 1, True, G // 2 - 1)

            pe.wait_ge(sem("a_ye"), count("a_ye", G * NT))
            pe.wait_ge(sem("d_ad"), count("d_ad", G))
            pe.wait_ge(sem("d_gate.0"), count("d_gate.0", 2))

            def project(c, tt):
                for hh in range(2):
                    last = mm(bank[2 * tt + hh][:], yT[:, c, tt * P:(tt + 1) * P],
                              wo_ssd[(c // 4) % 3][:, c % 4, hh * 512:(hh + 1) * 512], c, CT)
                return last

            for c4 in range(CT // 4 - 1):
                pe.wait_ge(sem(f"wo_in{c4}"), 16)
                for c in range(4 * c4, 4 * c4 + 4):
                    for tt in range(NT):
                        last = project(c, tt)
                last.then_inc(sem("pe_wo"), 1)
            pe.wait_ge(sem("wo_in0"), 32)
            for tt in range(NT):
                for c in range(CT - 4, CT):
                    last = project(c, tt)
                last.then_inc(sem("pe_wo"), 1)

            def moe(l):
                i = 1 + 2 * l
                gate(i, (2, 3))
                norm(i)
                hT_ready(i)
                pe.wait_ge(sem(f"rt_in.{l}"), count(f"rt_in.{l}", 64))
                for tt in range(NT):
                    for k in range(KD):
                        last = mm(bank[4][:, tt * 20:(tt + 1) * 20], hT[:, k, tt * P:(tt + 1) * P], rtw[:, k], k, KD)
                last.then_inc(sem(f"pe_rt.{l}"), 1)
                pe.wait_ge(sem(f"d_m.{l}"), count(f"d_m.{l}", 1))
                m2 = MM.rearrange("p t e -> p (t e)")
                pe.matmul(bank[5][:, 0:NT * NE], before[:], m2, start=True, stop=True)
                pe.matmul(bank[5][:, NT * NE:2 * NT * NE], ones[:], m2, start=True, stop=True).then_inc(sem(f"pe_rank.{l}"), 1)
                pe.wait_ge(sem(f"d_r.{l}"), count(f"d_r.{l}", 1))
                for n in range(8):
                    last = mm(bank[6][:, 0:NB], R[n], Bm[:, n, :], n, 8)
                last.then_inc(sem(f"pe_idx.{l}"), 1)

                def turn_rows(b, par, n):
                    pe.wait_ge(sem(f"gath{l}_{par}"), count(f"gath{l}_{par}", n * 16 + 16))
                    for hh in range(2):
                        if due(b):
                            pe.wait_ge(sem(f"t_ev{hh}.{l}"), count(f"t_ev{hh}.{l}", b))
                        for k in range(4):
                            kk_ = hh * 4 + k
                            last = pe.transpose(bank[hh][:, k * P:(k + 1) * P], xg[par][:, kk_:D:KD], ident[:])
                        last.then_inc(sem(f"pe_t.{l}"), 1)

                def up(b, par, n):
                    pe.wait_ge(sem(f"t_ev0.{l}"), count(f"t_ev0.{l}", b + 1))
                    pe.wait_ge(sem(f"t_ev1.{l}"), count(f"t_ev1.{l}", b + 1))
                    pe.wait_ge(sem(f"exp13_{par}.{l}"), count(f"exp13_{par}.{l}", n * 32 + 32))
                    if due(b - 1):
                        pe.wait_ge(sem(f"d_hid.{l}"), count(f"d_hid.{l}", b - 1))
                    for k in range(KD):
                        last = mm(bank[2 + par][:], xgT[par][:, k, :], w13[par][:, k, :], k, KD)
                    last.then_inc(sem(f"pe_h.{l}"), 1)

                def turn_hidden(b, par):
                    pe.wait_ge(sem(f"d_hid.{l}"), count(f"d_hid.{l}", b + 1))
                    if due(b):
                        pe.wait_ge(sem(f"a_ht.{l}"), count(f"a_ht.{l}", b))
                    for k in range(2):
                        last = pe.transpose(bank[4][:, k * P:(k + 1) * P], hid[:, k:FH:2], ident[:])
                    last.then_inc(sem(f"pe_ht.{l}"), 1)

                def down(b, par, n):
                    pe.wait_ge(sem(f"a_ht.{l}"), count(f"a_ht.{l}", b + 1))
                    pe.wait_ge(sem(f"exp2_{par}.{l}"), count(f"exp2_{par}.{l}", n * 16 + 16))
                    if due(b):
                        pe.wait_ge(sem(f"d_yo.{l}"), count(f"d_yo.{l}", b))
                    for hh in range(2):
                        for k in range(2):
                            last = mm(bank[6 + hh][:], hidT[:, k, :], w2s[par][:, k, hh * 512:(hh + 1) * 512], k, 2)
                    last.then_inc(sem(f"pe_o.{l}"), 1)

                pe.wait_ge(sem(f"d_idx.{l}"), count(f"d_idx.{l}", 1))
                turn_rows(0, 0, 0)
                up(0, 0, 0)
                turn_rows(1, 1, 0)
                up(1, 1, 0)
                turn_hidden(0, 0)
                turn_rows(2, 0, 1)
                down(0, 0, 0)

                def pair(i, turn_last):
                    for par in range(2):
                        b, n = i * 2 + par, i + par
                        up(b, par, i)
                        turn_hidden(b - 1, 1 - par)
                        if par == 0 or turn_last:
                            turn_rows(b + 1, 1 - par, n)
                        down(b - 1, 1 - par, n - 1)

                with pe.Fori(1, NE // 2 - 1) as i:
                    pair(i, True)
                pair(NE // 2 - 1, False)
                filling = overflow(pe, l)
                with pe.If(filling > 0):
                    turn_rows(NE, 0, NE // 2)
                with pe.Fori(NE // 2, (NB + 1) // 2) as i:
                    for par in range(2):
                        b, n = i * 2 + par, i + par
                        with filled(pe, 0, filling, b):
                            up(b, par, i)
                        with filled(pe, 1, filling, b):
                            turn_hidden(b - 1, 1 - par)
                        with filled(pe, -1, filling, b):
                            turn_rows(b + 1, 1 - par, n)
                        with filled(pe, 1, filling, b):
                            down(b - 1, 1 - par, n - 1)
                return filling

            pe.wait_ge(sem("x_up.1"), count("x_up.1", NT))
            pe.wait_ge(sem("d_late"), 2)
            ada_columns(late_sum[0])
            ada_columns(late_sum[1], KD).then_inc(sem("pe_ada"), 1)
            filling = moe(0)

            gate(2, (2, 3))
            norm(2)
            top_up(pe, filling, (("pe_t", 2), ("pe_h", 1), ("pe_ht", 1), ("pe_o", 1)))
            hT_ready(2)
            pe.wait_ge(sem("wqi_in"), 16 * 8)
            pe.wait_ge(sem("d_gate.2"), count("d_gate.2", 2))
            for j in range(5):
                if due(j - 1):
                    pe.wait_ge(sem("a_qi"), j - 1)
                for k in range(KD):
                    lw = wqi[:, k, j * P:(j + 1) * P] if j < 4 else kiw[:, k, :]
                    last = mm(bank[j % 2][:], lw, hT[:, k, :], k, KD)
                last.then_inc(sem("pe_qi"), 1)
            for tt in range(NT):
                for k in range(KD):
                    last = mm(bank[2][:, tt * IH:(tt + 1) * IH], hT[:, k, tt * P:(tt + 1) * P], wiw[:, k], k, KD)
            last.then_inc(sem("pe_wi"), 1)
            pe.wait_ge(sem("a_qi"), 5)

            def index(tt):
                w = (tt + 1) * P
                if tt > 2:
                    pe.wait_ge(sem("qk_ev"), 3 * (tt - 2))
                for h in range(IH):
                    n = (tt - 1) * IH + h
                    if due(n - 1):
                        pe.wait_ge(sem("a_rel"), n - 1)
                    rows = slice((h % 2) * HD, (h % 2 + 1) * HD)
                    pe.matmul(bank[6 + n % 2][:, 0:w], qiT[rows, h // 2, tt * P:(tt + 1) * P], kiT[rows, 0:w],
                              start=True, stop=True).then_inc(sem("pe_is"), 1)

            index(1)
            pe.wait_ge(sem("wq_in"), 32)
            pe.wait_ge(sem("wkv_in"), 16)
            pe.wait_ge(sem("d_wi"), 1)

            def turn_qk(tt):
                pe.wait_ge(sem("d_qkn"), tt + 1)
                pe.wait_ge(sem("a_rel"), IH * min(tt + 2, NT - 1))
                for gi in range(3):
                    n = 3 * tt + gi
                    if due(n - 1):
                        pe.wait_ge(sem("qk_ev"), n - 1)
                    for i in range(4):
                        src = qkn[:, (gi * 4 + i) * P:(gi * 4 + i + 1) * P]
                        last = pe.transpose(bank[6 + n % 2][:, i * P:(i + 1) * P], src, ident[:])
                    last.then_inc(sem("pe_qk"), 1)

            for tt in range(NT):
                b0 = 3 * (tt % 2)
                if due(tt - 1):
                    pe.wait_ge(sem("d_qkn"), tt - 1)
                if due(tt - 1):
                    pe.wait_ge(sem("a_v"), tt - 1)
                for i in range(3):
                    for k in range(KD):
                        last = mm(bank[b0 + i][:], hT[:, k, tt * P:(tt + 1) * P], (wq[0], wq[1], wkv)[i][:, k, :], k, KD)
                last.then_inc(sem("pe_qkv"), 1)
                if tt == 0:
                    index(2)
                else:
                    turn_qk(tt - 1)
                if tt == 1:
                    index(3)
            turn_qk(NT - 1)
            pe.wait_ge(sem("qk_ev"), 12)

            def scores(u):
                tt, kv = u // 4, u % 4
                w = (tt + 1) * P
                for i in range(4):
                    h = 4 * kv + i
                    rows = slice((h % 2) * HD, (h % 2 + 1) * HD)
                    if u > 0:
                        pe.wait_ge(sem("d_sm"), 4 * (u - 1) + i + 1)
                    pe.matmul(bank[i][:, 0:w], qT[rows, h // 2, tt * P:(tt + 1) * P], kT[rows, kv, 0:w],
                              start=True, stop=True).then_inc(sem("pe_s"), 1)

            def attend(u):
                tt, kv = u // 4, u % 4
                base = chunks_before(u)
                if u % 4 == 0:
                    if due(2 * tt):
                        pe.wait_ge(sem("d_xo"), 2 * tt)
                pe.wait_ge(sem("a_exp"), 4 * u + 4)
                for c in range(tt + 1):
                    n = base + c
                    if due(n // 2):
                        pe.wait_ge(sem(("a_pt", "d_pt")[n % 2]), n // 2)
                    for i in range(4):
                        last = pe.transpose(bank[4 + n % 2][:, i * P:(i + 1) * P], Sm[u % 2][:, i, c * P:(c + 1) * P], ident[:])
                    last.then_inc(sem("pe_pt"), 1)
                pe.wait_ge(sem("a_pt"), (base + tt + 2) // 2)
                if due((base + tt + 1) // 2):
                    pe.wait_ge(sem("d_pt"), (base + tt + 1) // 2)
                for i in range(4):
                    h = 4 * kv + i
                    for c in range(tt + 1):
                        last = mm(bank[6 + h // 8][:, (h % 8) * HD:(h % 8 + 1) * HD], PT[:, c, i * P:(i + 1) * P],
                                  V[:, c, kv * HD:(kv + 1) * HD], c, tt + 1)
                last.then_inc(sem("pe_pv"), 1)

            def project_out(tt):
                pe.wait_ge(sem("d_o"), tt + 1)
                for hh in range(2):
                    for i in range(4):
                        last = pe.transpose(bank[4 + hh][:, i * P:(i + 1) * P],
                                            o[:, (hh * 4 + i) * P:(hh * 4 + i + 1) * P], ident[:])
                    last.then_inc(sem("pe_ot"), 1)
                pe.wait_ge(sem("ot_ev"), 2 * tt + 2)
                pe.wait_ge(sem("wo_dsa_in"), 16)
                for hh in range(2):
                    for k in range(KD):
                        last = mm(bank[6 + hh][:], oT[:, k, :], wo_dsa[:, k, hh * 512:(hh + 1) * 512], k, KD)
                    last.then_inc(sem("pe_xo"), 1)

            scores(0)
            for u in range(16):
                if u < 15:
                    scores(u + 1)
                attend(u)
                if u % 4 == 3:
                    project_out(u // 4)
            pe.wait_ge(sem("d_xo"), 8)
            moe(1)

        @block.scalar
        def _(act):
            credit(act, [n for n in CREDIT if n[0] == "a"])
            def copy(out, in_):
                return act.activation(out, in_, ACT.Copy)

            def squares(i):
                for tt in range(NT):
                    if i > 0:
                        act.wait_ge(sem("x_up"), (i - 1) * NT + tt + 1)
                    act.activation(xn[:, tt], x[:, tt], ACT.Square, accum_out=ssq[:, i, tt:tt + 1]).then_inc(sem(f"n_sq.{i}"), 1)

            def norm(i):
                act.wait_ge(sem(f"n_col.{i}"), count(f"n_col.{i}", 1))
                for k in range(1, KD, 2):
                    act.wait_ge(sem(f"n_tr.{i}"), count(f"n_tr.{i}", k + 1))
                    act.activation(hT[:, k, :], bank[1][:], ACT.Identity, bias=modcol[:, 3 * i, k:k + 1],
                                   scale=acol[:, i, k:k + 1]).then_inc(sem(f"n_ev1.{i}"), 1)

            act.dma_start(ccol[:], t["c"][0].rearrange("(p k) -> p k", k=KD)).then_inc(sem("c_in"), 16)
            s = sem("par_in")
            act.dma_start(dtw, w_in[:, :, OFF_DT:OFF_DT + HEADS]).then_inc(s, 16)
            act.dma_start(adab[:], t["ada_b"].rearrange("l (j p k) -> p (l j) k", j=6, k=KD)).then_inc(s, 16)
            act.dma_start(normw[:, 0:4:2], t["norm_mix"].rearrange("l (p k) -> p l k", k=KD)).then_inc(s, 16)
            act.dma_start(normw[:, 1:4:2], t["norm_ffn"].rearrange("l (p k) -> p l k", k=KD)).then_inc(s, 16)
            act.dma_start(dtb, row_bc(t["ssd_dt_bias"][0], HEADS)).then_inc(s, 16)
            act.dma_start(alog, row_bc(t["ssd_a_log"][0], HEADS)).then_inc(s, 16)
            act.dma_start(dsk, row_bc(t["ssd_d"][0], HEADS)).then_inc(s, 16)
            act.dma_start(prow, t["ssd_conv_w"][0].rearrange("a (c p) -> (a c) p", p=P)).then_inc(s, 16)
            act.dma_start(brow[0:CONV_TILES, :], t["ssd_conv_b"][0].rearrange("(c p) -> c p", p=P)).then_inc(s, 16)
            act.dma_start(brow[CONV_TILES:CONV_TILES + CT, :], t["ssd_norm"][0].rearrange("(c p) -> c p", p=P)).then_inc(s, 16)
            act.wait_ge(sem("c_in"), 16)
            act.activation(cond[:], ccol[:], ACT.Tanh, scale=0.5).then_inc(sem("a_c"), 1)
            act.wait_ge(sem("x_in"), 16)
            squares(0)
            norm(0)
            act.wait_ge(sem("d_v"), 1)
            act.activation(s2, s2, ACT.Exp)
            act.activation(alog, alog, ACT.Exp).then_inc(sem("a_dt"), 1)

            def conv_in(gn, par, j):
                n = gn * NT + j
                if j == 0:
                    act.wait_ge(sem("p_gp"), gn + 1)
                act.wait_ge(sem("pe_x"), n + 1)
                if due(n - 1):
                    act.wait_ge(sem("d_mu"), count("d_mu", n - 1))
                copy(upad[j % 2][:, 3:515], bank[j % 2][:])
                act.activation(cacc[j % 2], bank[j % 2][:], ACT.Identity, bias=gp[par][:, j, 4:5],
                               scale=gp[par][:, j, 3:4]).then_inc(sem("a_xe"), 1)

            def conv_tanh(gn, j):
                n = gn * NT + j
                act.wait_ge(sem("d_cv"), n + 1)
                act.activation(th[j % 2], cacc[j % 2], ACT.Tanh).then_inc(sem("a_th"), 1)

            def z_tanh(gn, j):
                n = gn * NT + j
                act.wait_ge(sem("pe_z"), n + 1)
                if due(n):
                    act.wait_ge(sem("d_zs"), n)
                act.activation(zt, bank[2][:, 0:GC], ACT.Tanh, scale=0.5).then_inc(sem("a_zt"), 1)

            conv_in(0, 0, 0)
            conv_in(0, 0, 1)
            z_tanh(0, 0)
            act.wait_ge(sem("d_cs"), 1)
            act.activation(ea, acs, ACT.Exp)
            act.activation(dte, dte, ACT.Exp)
            act.activation(s3, s3, ACT.Exp)
            act.drain().then_inc(sem("a_dec"), 1)
            conv_tanh(0, 0)
            z_tanh(0, 1)
            conv_tanh(0, 1)
            for j in range(2, NT):
                conv_in(0, 0, j)
                z_tanh(0, j)
                conv_tanh(0, j)

            def group(g, par, last):
                for j in range(NT):
                    m = g * NT + j
                    act.wait_ge(sem("pe_df"), count("pe_df", m + 1))
                    if due(m):
                        act.wait_ge(sem("d_w"), count("d_w", m))
                    act.activation(decay.rearrange("p h l -> p (h l)"), bank[4][:], ACT.Exp).then_inc(sem("a_ex"), 1)
                    if not last:
                        conv_in(g + 1, 1 - par, j)
                    if j > 0:
                        y_out(g, par, j - 1)
                    act.wait_ge(sem("p_y"), count("p_y", m + 1))
                    if due(m):
                        act.wait_ge(sem("pe_yt"), count("pe_yt", m))
                    act.activation(yn, yb, ACT.Square, scale=0.5 * GC ** -0.5, accum_out=yss).then_inc(sem("a_sq"), 1)
                    if not last:
                        z_tanh(g + 1, j)
                        conv_tanh(g + 1, j)
                    act.wait_ge(sem("p_rs"), m + 1)
                    act.activation(yn, yb, ACT.Copy, scale=yrs).then_inc(sem("a_yn"), 1)
                y_out(g, par, NT - 1)

            def y_out(g, par, j):
                act.wait_ge(sem("pe_yt"), count("pe_yt", g * NT + j + 1))
                for i in range(2):
                    act.activation(yT[:, bass.DynSlice(g * 2 + i, 1), j * P:(j + 1) * P],
                                   bank[4][:, i * P:(i + 1) * P].unsqueeze(1), ACT.Copy, scale=gn_w[par][:, i:i + 1])
                act.drain().then_inc(sem("a_ye"), 1)

            with act.Fori(0, G // 2 - 1) as i:
                group(i * 2, 0, False)
                group(i * 2 + 1, 1, False)
            group(G - 2, 0, False)
            group(G - 1, 1, True)

            def moe(l):
                i = 1 + 2 * l
                squares(i)
                act.wait_ge(sem(f"x_up.{i}"), count(f"x_up.{i}", NT))
                s = sem(f"rt_in.{l}")
                act.dma_start(rtw[:, :, 0:NG], t["moe_w_group"][l].rearrange("(p k) n -> p k n", k=KD)).then_inc(s, 16)
                act.dma_start(rtw[:, :, NG:], t["moe_w_expert"][l].rearrange("(p k) n -> p k n", k=KD)).then_inc(s, 16)
                act.dma_start(rtb[:, 0:NG], row_bc(t["moe_b_group"][l], NG)).then_inc(s, 16)
                act.dma_start(rtb[:, NG:], row_bc(t["moe_b_expert"][l], NE)).then_inc(s, 16)
                act.wait_ge(sem("rows_set"), 16 * -(-OVER * P // SEQ))
                act.wait_ge(sem(f"n_xn.{i}"), count(f"n_xn.{i}", NT))
                act.dma_start(xn_dram[l].rearrange("(t p) d -> p t d", p=P), xn[:]).then_inc(sem(f"xn_stored.{l}"), 16)
                norm(i)
                act.wait_ge(sem(f"d_g.{l}"), count(f"d_g.{l}", 1))
                act.activation(gsh, gsh, ACT.Exp).then_inc(sem(f"a_r.{l}"), 1)
                act.wait_ge(sem(f"d_e.{l}"), count(f"d_e.{l}", 1))
                act.activation(g2, g2, ACT.Exp).then_inc(sem(f"a_r.{l}"), 1)

                def turned(b, par):
                    act.wait_ge(sem(f"pe_t.{l}"), count(f"pe_t.{l}", b * 2 + 2))
                    if due(b - 1):
                        act.wait_ge(sem(f"pe_h.{l}"), count(f"pe_h.{l}", b - 1))
                    for k in range(4):
                        act.activation(xgT[par][:, 4 + k, :], bank[1][:, k * P:(k + 1) * P], ACT.Identity,
                                       bias=modcol[:, 3 * i, 4 + k:5 + k], scale=acol[:, i, 4 + k:5 + k])
                    act.drain().then_inc(sem(f"t_ev1.{l}"), 1)

                def gate_tanh(b, par):
                    act.wait_ge(sem(f"pe_h.{l}"), count(f"pe_h.{l}", b + 1))
                    if due(b):
                        act.wait_ge(sem(f"d_hid.{l}"), count(f"d_hid.{l}", b))
                    act.activation(mth, bank[2 + par][:, 0:FH], ACT.Tanh, scale=0.5).then_inc(sem(f"a_mt.{l}"), 1)

                def hidden_turned(b):
                    act.wait_ge(sem(f"pe_ht.{l}"), count(f"pe_ht.{l}", b + 1))
                    if due(b):
                        act.wait_ge(sem(f"pe_o.{l}"), count(f"pe_o.{l}", b))
                    copy(hidT.rearrange("p a b -> p (a b)"), bank[4][:, 0:2 * P]).then_inc(sem(f"a_ht.{l}"), 1)

                def result(b, par):
                    act.wait_ge(sem(f"d_yo.{l}"), count(f"d_yo.{l}", b + 1))
                    act.dma_start(y_dram.rearrange("(b p) d -> b p d", p=P)[bass.DynSlice(b, 1)].rearrange("o p d -> (o p) d"),
                                  yo[par]).then_inc(sem(f"y_stored_{par}.{l}"), 16)

                act.wait_ge(sem(f"d_idx.{l}"), count(f"d_idx.{l}", 1))
                turned(0, 0)
                gate_tanh(0, 0)
                turned(1, 1)
                gate_tanh(1, 1)
                hidden_turned(0)
                turned(2, 0)
                result(0, 0)

                def pair(i, turn_last):
                    for par in range(2):
                        b = i * 2 + par
                        gate_tanh(b, par)
                        hidden_turned(b - 1)
                        if par == 0 or turn_last:
                            turned(b + 1, 1 - par)
                        result(b - 1, 1 - par)

                with act.Fori(1, NE // 2 - 1) as ii:
                    pair(ii, True)
                pair(NE // 2 - 1, False)
                filling = overflow(act, l)
                with act.If(filling > 0):
                    turned(NE, 0)
                with act.Fori(NE // 2, (NB + 1) // 2) as ii:
                    for par in range(2):
                        b = ii * 2 + par
                        with filled(act, 0, filling, b):
                            gate_tanh(b, par)
                        with filled(act, 1, filling, b):
                            hidden_turned(b - 1)
                        with filled(act, -1, filling, b):
                            turned(b + 1, 1 - par)
                        with filled(act, 1, filling, b):
                            result(b - 1, 1 - par)
                return filling

            filling = moe(0)

            squares(2)
            top_up(act, filling, (("t_ev1", 1), ("a_mt", 1), ("a_ht", 1), ("y_stored_{par}", 16)))
            norm(2)
            for j in range(5):
                act.wait_ge(sem("pe_qi"), j + 1)
                copy(qiT[:, j, :] if j < 4 else kiT, bank[j % 2][:]).then_inc(sem("a_qi"), 1)

            def rectify(tt):
                w = (tt + 1) * P
                for h in range(IH):
                    n = (tt - 1) * IH + h
                    act.wait_ge(sem("pe_is"), n + 1)
                    if due(n - 1):
                        act.wait_ge(sem("d_acc"), n - 1)
                    act.activation(rel[n % 2][:, 0:w], bank[6 + n % 2][:, 0:w], ACT.Relu, scale=HD ** -0.5).then_inc(sem("a_rel"), 1)

            def turned_qk(tt):
                for gi in (0, 1, 2):
                    n = 3 * tt + gi
                    act.wait_ge(sem("pe_qk"), n + 1)
                    dst = qT[:, 4 * gi:4 * gi + 4, tt * P:(tt + 1) * P] if gi < 2 else kT[:, :, tt * P:(tt + 1) * P]
                    act.activation(dst, bank[6 + n % 2][:].rearrange("p (a b) -> p a b", b=P), ACT.Copy,
                                   scale=qkw[:, gi // 2:gi // 2 + 1]).then_inc(sem("qk_ev"), 1)

            rectify(1)
            for tt in range(NT):
                b0 = 3 * (tt % 2)
                act.wait_ge(sem("pe_qkv"), tt + 1)
                if due(tt):
                    act.wait_ge(sem("d_hss"), tt)
                act.activation(sqs[:, 0:512], bank[b0][:], ACT.Square)
                act.activation(sqs[:, 512:1024], bank[b0 + 1][:], ACT.Square)
                act.activation(sqs[:, 1024:1280], bank[b0 + 2][:, 0:256], ACT.Square)
                copy(V[:, tt, :], bank[b0 + 2][:, 256:512]).then_inc(sem("a_v"), 1)
                act.drain().then_inc(sem("a_sqs"), 1)
                if tt == 0:
                    rectify(2)
                else:
                    turned_qk(tt - 1)
                if tt == 1:
                    rectify(3)
            turned_qk(NT - 1)
            for u in range(16):
                tt, kv = u // 4, u % 4
                w = (tt + 1) * P
                base = chunks_before(u)
                act.wait_ge(sem("d_nmx"), u + 1)
                for i in range(4):
                    act.activation(Sm[u % 2][:, i, 0:w], Sm[u % 2][:, i, 0:w], ACT.Exp, bias=nmx[:, kv, i:i + 1],
                                   accum_out=rsum[:, tt % 2, 4 * kv + i:4 * kv + i + 1]).then_inc(sem("a_exp"), 1)
                for c in range(tt + 1):
                    if (base + c) % 2 == 0:
                        act.wait_ge(sem("pe_pt"), base + c + 1)
                        if due(u):
                            act.wait_ge(sem("pe_pv"), u)
                        copy(PT[:, c, :], bank[4][:]).then_inc(sem("a_pt"), 1)
                if kv == 3:
                    for hh in range(2):
                        act.wait_ge(sem("pe_ot"), 2 * tt + hh + 1)
                        copy(oT[:, 4 * hh:4 * hh + 4, :].rearrange("p a b -> p (a b)"), bank[4 + hh][:]).then_inc(sem("ot_ev"), 1)
            moe(1)

        @block.vector
        def _(dve):
            credit(dve, [n for n in CREDIT if n[0] == "d"])
            def tt_(out, a, b, op):
                dve.tensor_tensor(out, a, b, op)
                dve.drain()

            def ts_(out, a, s1_, s2_, op0, op1=ALU.bypass):
                if s2_ is None:
                    dve.tensor_scalar(out, a, s1_, None, op0)
                else:
                    dve.tensor_scalar(out, a, s1_, s2_, op0, op1)
                dve.drain()

            def stt(out, a, s, b, op0, op1):
                return dve.scalar_tensor_tensor(out=out, in0=a, scalar=s, in1=b, op0=op0, op1=op1)

            def red(out, a, op):
                dve.tensor_reduce(out, a, AX.X, op)
                dve.drain()

            def ada_sum(buf, chunks, out=None):
                for k in chunks:
                    if k == 0:
                        ins = dve.tensor_scalar(buf[:, 0], buf[:, 0], cond[:, 0:1], None, ALU.mult)
                    else:
                        ins = stt(out if k == KD - 1 and out is not None else buf[:, 0], buf[:, k], cond[:, k:k + 1],
                                  buf[:, 0], ALU.mult, ALU.add)
                    if k < KD - 1:
                        dve.drain()
                return ins

            def ada_out(i, at=0):
                return dve.tensor_tensor(modcol[:, i, :], bank[7][:, GC + at:GC + at + KD], adab[:, i, :], ALU.add)

            def norm(i):
                dve.wait_ge(sem(f"n_rs.{i}"), count(f"n_rs.{i}", 1))
                for tt in range(NT):
                    dve.tensor_scalar(xn[:, tt], x[:, tt], rstd[:, i, tt:tt + 1], None, ALU.mult).then_inc(sem(f"n_xn.{i}"), 1)
                if i == 0:
                    first_pieces()
                dve.drain()
                stt(acol[:, i], modcol[:, 3 * i + 1], 1.0, normw[:, i], ALU.add, ALU.mult).then_inc(sem(f"n_col.{i}"), 1)
                dve.drain()
                for k in range(0, KD, 2):
                    dve.wait_ge(sem(f"n_tr.{i}"), count(f"n_tr.{i}", k + 1))
                    dve.tensor_scalar(hT[:, k, :], bank[0][:], acol[:, i, k:k + 1], modcol[:, 3 * i, k:k + 1],
                                      ALU.mult, ALU.add).then_inc(sem(f"n_ev0.{i}"), 1)

            def gate(i, banks, dst):
                for hh in range(2):
                    dve.wait_ge(sem(f"pe_gate.{i}"), count(f"pe_gate.{i}", hh + 1))
                    dve.tensor_copy(dst.rearrange("p (q k) -> p k q", k=KD)[:, 4 * hh:4 * hh + 4, :],
                                    bank[banks[hh]][:].rearrange("p (k q) -> p k q", k=4)).then_inc(sem(f"d_gate.{i}"), 1)

            def first_pieces():
                for n in range(2):
                    for q in range(4):
                        dve.wait_ge(sem(f"ada_first{n}{q}"), 16)
                        ins = ada_sum(ada[n], range(2 * q, 2 * q + 2))
                    ins.then_inc(sem("d_first"), 1)
                dve.wait_ge(sem("par_in"), 160)
                for n in range(2):
                    dve.wait_ge(sem("pe_ada"), n + 1)
                    ada_out(n).then_inc(sem("d_ada"), 1)

            dve.wait_ge(sem("a_c"), 1)
            stt(cond[:], cond[:], 1.0, ccol[:], ALU.add, ALU.mult)
            dve.drain()
            ts_(cond[:], cond[:], 0.5, None, ALU.mult)
            norm(0)
            dve.wait_ge(sem("pe_par"), 1)
            dve.tensor_scalar(cwT.rearrange("p a c -> p (a c)"), bank[2][:, 0:160], 0.5, None, ALU.mult)
            dve.tensor_scalar(nwT, bank[2][:, 160:160 + CT], 0.5, None, ALU.mult)
            dve.drain().then_inc(sem("d_par"), 1)
            dve.wait_ge(sem("pe_dt"), 1)
            tt_(s1, bank[3][:, 0:P].rearrange("p (c h) -> p c h", h=HEADS), rep(dtb, NT), ALU.add)
            ts_(s3, s1, -1.0, None, ALU.mult)
            dve.tensor_tensor(s2, s1, s3, ALU.min).then_inc(sem("d_v"), 1)
            ts_(s1, s1, 0.0, None, ALU.max)
            dve.wait_ge(sem("a_dt"), 1)
            ts_(s3, s2, 2.0, None, ALU.add)
            dve.reciprocal(s3, s3)
            dve.drain()
            tt_(s2, s2, s3, ALU.mult)
            tt_(s3, s2, s2, ALU.mult)
            ts_(dt, s3, 1.0 / (2 * LOG1P_TERMS + 1), 1.0 / (2 * LOG1P_TERMS - 1), ALU.mult, ALU.add)
            for n in range(LOG1P_TERMS - 2, -1, -1):
                tt_(dt, dt, s3, ALU.mult)
                ts_(dt, dt, 1.0 / (2 * n + 1), None, ALU.add)
            tt_(dt, dt, s2, ALU.mult)
            stt(dt, dt, 2.0, s1, ALU.mult, ALU.add)
            dve.drain()
            stt(aa, dt, -1.0, rep(alog, NT), ALU.mult, ALU.mult).then_inc(sem("d_a"), 1)
            dve.wait_ge(sem("pe_cs"), 1)
            a2 = bank[4][:, 0:P].rearrange("p (c h) -> p c h", h=HEADS)
            last2 = bank[4][:, P:2 * P].rearrange("p (c h) -> p c h", h=HEADS)
            dve.tensor_copy(acs, a2)
            dve.tensor_copy(s3, last2)
            dve.drain()
            dve.tensor_tensor(dte, s3, acs, ALU.subtract)
            dve.drain().then_inc(sem("d_cs"), 1)
            dve.wait_ge(sem("a_dec"), 1)
            dve.drain().then_inc(sem("d_dt"), 1)

            def conv(gn, par, j):
                n = gn * NT + j
                dve.wait_ge(sem("a_xe"), n + 1)
                for k in range(3):
                    ins = stt(cacc[j % 2], upad[j % 2][:, k:k + SEQ], gp[par][:, j, k:k + 1], cacc[j % 2], ALU.mult, ALU.add)
                    if k < 2:
                        dve.drain()
                ins.then_inc(sem("d_cv"), 1)

            def conv_silu(gn, par, j):
                n = gn * NT + j
                dve.wait_ge(sem("a_th"), n + 1)
                stt(xbcT[par][:, j, :], th[j % 2], 1.0, cacc[j % 2], ALU.add, ALU.mult).then_inc(sem("d_mu"), 1)

            def z_silu(gn, par, j):
                n = gn * NT + j
                dve.wait_ge(sem("a_zt"), n + 1)
                stt(zs[par][:, j], zt, 1.0, bank[2][:, 0:GC], ALU.add, ALU.mult).then_inc(sem("d_zs"), 1)

            for j in range(NT):
                conv(0, 0, j)
                z_silu(0, 0, j)
                conv_silu(0, 0, j)

            def heads(ap):
                return ap.rearrange("p (h d) -> p h d", d=HD)

            def group(g, par, last):
                hs = bass.DynSlice(g * JH, JH)
                for j in range(NT):
                    m = g * NT + j
                    dve.wait_ge(sem("pe_xt"), m + 1)
                    dve.tensor_tensor(heads(xdt), heads(bank[3][:, 0:GC]), bc(dt[:, j, hs], HD), ALU.mult).then_inc(sem("d_xdt"), 1)
                    if due(m):
                        dve.wait_ge(sem("p_y"), count("p_y", m))
                    dve.tensor_tensor(heads(skip), heads(bank[3][:, 0:GC]), bc(dsk[:, hs], HD), ALU.mult).then_inc(sem("d_skip"), 1)
                    if j < NT - 1:
                        if due(g * (NT - 1) + j):
                            dve.wait_ge(sem("pe_st"), count("pe_st", g * (NT - 1) + j))
                        dve.tensor_copy(btok, bank[3][:, 2 * P:3 * P]).then_inc(sem("d_bt"), 1)
                    dve.wait_ge(sem("pe_cb"), m + 1)
                    dve.tensor_tensor(cbm, bank[5][:, 0:P], upto[:], ALU.mult).then_inc(sem("d_cb"), 1)
                    dve.drain()
                    dve.wait_ge(sem("a_ex"), count("a_ex", m + 1))
                    dve.tensor_tensor(wmat, decay, rep(cbm, JH), ALU.mult).then_inc(sem("d_w"), 1)
                    dve.wait_ge(sem("pe_y"), m + 1)
                    if due(m):
                        dve.wait_ge(sem("a_yn"), count("a_yn", m))
                    if j == 0:
                        dve.tensor_copy(yb, bank[6][:, 0:GC]).then_inc(sem("d_y"), 1)
                    else:
                        dve.tensor_tensor(heads(yb), heads(bank[6][:, GC:2 * GC]), bc(ea[:, j, hs], HD), ALU.mult)
                        dve.drain()
                        dve.tensor_tensor(yb, yb, bank[6][:, 0:GC], ALU.add).then_inc(sem("d_y"), 1)
                    if j == 0:
                        dve.wait_ge(sem("pe_st"), count("pe_st", g * (NT - 1) + j + 1))
                        dve.tensor_copy(state, bank[7][:, 0:GC]).then_inc(sem("d_st"), 1)
                    elif j < NT - 1:
                        dve.tensor_tensor(heads(state), heads(state), bc(s3[:, j, hs], HD), ALU.mult)
                        dve.drain()
                        dve.wait_ge(sem("pe_st"), count("pe_st", g * (NT - 1) + j + 1))
                        dve.tensor_tensor(state, state, bank[7][:, 0:GC], ALU.add).then_inc(sem("d_st"), 1)
                    if not last:
                        conv(g + 1, 1 - par, j)
                        z_silu(g + 1, 1 - par, j)
                        conv_silu(g + 1, 1 - par, j)
                    elif j == 0:
                        gate(0, (0, 1), gatebc0)
                    if j == 0:
                        dve.wait_ge(sem("ada_in"), g * 16 + 16)
                        ada_sum(ada[0], range(0, 3))
                    if j == 1:
                        ada_sum(ada[0], range(3, 6))
                    if j == 2:
                        ada_sum(ada[0], range(6, KD)).then_inc(sem("d_ps"), 1)
                dve.wait_ge(sem("pe_ad"), g + 1)
                dve.tensor_tensor(modcol[:, bass.DynSlice(g + 2, 1), :], bank[7][:, GC:GC + KD].unsqueeze(1),
                                  adab[:, bass.DynSlice(g + 2, 1), :], ALU.add).then_inc(sem("d_ad"), 1)

            with dve.Fori(0, G // 2 - 1) as i:
                group(i * 2, 0, False)
                group(i * 2 + 1, 1, False)
            group(G - 2, 0, False)
            group(G - 1, 1, True)
            dve.wait_ge(sem("p_y"), count("p_y", G * NT))
            for n in range(2):
                dve.wait_ge(sem("ada_in"), 16 * (G + 1 + n))
                ada_sum(ada[0], range(KD), late_sum[n]).then_inc(sem("d_late"), 1)
            for tt in range(NT):
                dve.wait_ge(sem("pe_wo"), 3 + tt + 1)
                for hh in range(2):
                    half = slice(hh * 512, (hh + 1) * 512)
                    dve.tensor_tensor(xn[:, tt, half], bank[2 * tt + hh][:], gatebc0[:, half], ALU.mult)
                dve.drain()
                dve.tensor_tensor(x[:, tt], x[:, tt], xn[:, tt], ALU.add).then_inc(sem("x_up.1"), 1)

            def onehot(dst, vals, mx):
                red(mx, vals, ALU.max)
                tt_(cand, vals, bc(mx, 4), ALU.is_equal)
                tt_(cand, cand, pref[:], ALU.mult)
                red(g3, cand, ALU.max)
                tt_(dst, cand, bc(g3, 4), ALU.is_equal)

            def moe(l):
                i = 1 + 2 * l
                if l == 0:
                    dve.wait_ge(sem("pe_ada"), 3)
                    ada_out(10)
                    ada_out(11, KD)
                gate(i, (2, 3), gatebc)
                norm(i)
                dve.wait_ge(sem(f"pe_rt.{l}"), count(f"pe_rt.{l}", 1))
                dve.wait_ge(sem(f"rt_in.{l}"), count(f"rt_in.{l}", 64))
                tt_(lg, bank[4][:, 0:80].rearrange("p (t e) -> p t e", e=20), rep(rtb, NT), ALU.add)
                onehot(goh, lg[:, :, 0:NG], mx1)
                dve.tensor_tensor(gsh, lg[:, :, 0:NG], bc(mx1, 4), ALU.subtract).then_inc(sem(f"d_g.{l}"), 1)
                by_group = [P, NT, NG, EG]
                group = goh.unsqueeze(3).broadcast_to(by_group)
                tt_(prod.rearrange("p t (g e) -> p t g e", e=EG),
                    lg[:, :, NG:].rearrange("p t (g e) -> p t g e", e=EG), group, ALU.mult)
                red(ein, prod.rearrange("p t (g e) -> p t e g", e=EG), ALU.add)
                onehot(oh1, ein, mx1)
                stt(m4, oh1, NEG, ein, ALU.mult, ALU.add)
                dve.drain()
                onehot(oh2, m4, mx2)
                dve.tensor_tensor(g2, mx2, mx1, ALU.subtract).then_inc(sem(f"d_e.{l}"), 1)
                for c, oh in ((0, oh1), (1, oh2)):
                    dve.tensor_tensor(M[:, c].rearrange("p t (g e) -> p t g e", e=EG),
                                      oh.unsqueeze(2).broadcast_to(by_group), group, ALU.mult)
                dve.memset(toff[:, 0], 0.0)
                dve.drain()
                dve.tensor_tensor(MM, M[:, 0], M[:, 1], ALU.add).then_inc(sem(f"d_m.{l}"), 1)
                dve.tensor_tensor(picked[1], M, iota[:, 0:NE].unsqueeze(1).unsqueeze(1).broadcast_to([P, 2, NT, NE]), ALU.mult)
                dve.drain()
                red(blk, picked[1], ALU.add)
                dve.wait_ge(sem(f"pe_rank.{l}"), count(f"pe_rank.{l}", 1))
                cnt = bank[5][:, NT * NE:2 * NT * NE].rearrange("p (t e) -> p t e", e=NE)
                for tt in range(1, NT):
                    tt_(toff[:, tt], toff[:, tt - 1], cnt[:, tt - 1], ALU.add)
                tt_(tot, toff[:, NT - 1], cnt[:, NT - 1], ALU.add)
                tt_(rank, toff, bank[5][:, 0:NT * NE].rearrange("p (t e) -> p t e", e=NE), ALU.add)
                ts_(over, tot, float(P), None, ALU.is_gt)
                for c in (2, 3):
                    stt(over, tot, float(c * P), over, ALU.is_gt, ALU.add)
                    dve.drain()
                dve.tensor_tensor_scan(cumi, ones[:, 0:NE], over, 0.0, ALU.mult, ALU.add)
                dve.drain()
                tt_(base2, cumi, over, ALU.subtract)
                ts_(base2, base2, float(NE - 1), None, ALU.add)
                dve.tensor_tensor(picked[0], M, rank.unsqueeze(1).broadcast_to([P, 2, NT, NE]), ALU.mult)
                dve.tensor_tensor(picked[2], M, base2.unsqueeze(1).unsqueeze(1).broadcast_to([P, 2, NT, NE]), ALU.mult)
                dve.drain()
                dve.tensor_reduce(slf, picked[2], AX.X, ALU.add)
                red(rr, picked[0], ALU.add)
                ts_(kk, rr, float(P), None, ALU.is_ge)
                tt_(slf, slf, blk, ALU.subtract)
                tt_(slf, slf, kk, ALU.mult)
                for c in (2, 3):
                    stt(kk, rr, float(c * P), kk, ALU.is_ge, ALU.add)
                    dve.drain()
                tt_(blk, blk, slf, ALU.add)
                tt_(blk, blk, kk, ALU.add)
                stt(rmod, kk, -float(P), rr, ALU.mult, ALU.add)
                dve.drain()
                for c in range(2):
                    for tt in range(NT):
                        n = c * NT + tt
                        dve.tensor_scalar(R[n], iota[:], rmod[:, c, tt:tt + 1], None, ALU.is_equal)
                        dve.tensor_scalar(Bm[:, n, :], iota[:, 0:NB], blk[:, c, tt:tt + 1], tokid[:, tt:tt + 1],
                                          ALU.is_equal, ALU.mult)
                dve.drain().then_inc(sem(f"d_r.{l}"), 1)
                dve.wait_ge(sem(f"pe_idx.{l}"), count(f"pe_idx.{l}", 1))
                dve.tensor_copy(idx, bank[6][:, 0:NB]).then_inc(sem(f"d_idx.{l}"), 1)
                tt_(ovt[0:1], rep(cumi[0:1, :], OVER), bc(iota[0:1, 0:OVER], NE), ALU.is_le)
                red(ovf[0:1], ovt[0:1], ALU.add)
                ts_(ovf[0:1], ovf[0:1], float(NE - 1), None, ALU.min)
                dve.tensor_copy(ovi[0:1, 0:OVER], ovf[0:1])
                dve.tensor_copy(ovi[0:1, OVER:OVER + 1], cumi[0:1, NE - 1:NE])
                dve.drain().then_inc(sem(f"over_ids.{l}"), 1)
                stt(slf, blk, float(P), rmod, ALU.mult, ALU.add)
                dve.drain()
                dve.tensor_copy(sloti, slf)
                dve.wait_ge(sem(f"a_r.{l}"), count(f"a_r.{l}", 2))
                red(g1, gsh, ALU.add)
                ts_(g3, g2, 1.0, None, ALU.add)
                tt_(g1, g1, g3, ALU.mult)
                dve.reciprocal(g1, g1)
                dve.drain()
                ts_(wc1, g1, 0.5, None, ALU.mult)
                tt_(wc2, wc1, g2, ALU.mult)

                def turned(b, par):
                    dve.wait_ge(sem(f"pe_t.{l}"), count(f"pe_t.{l}", b * 2 + 1))
                    if due(b - 1):
                        dve.wait_ge(sem(f"pe_h.{l}"), count(f"pe_h.{l}", b - 1))
                    for k in range(4):
                        dve.tensor_scalar(xgT[par][:, k, :], bank[0][:, k * P:(k + 1) * P], acol[:, i, k:k + 1],
                                          modcol[:, 3 * i, k:k + 1], ALU.mult, ALU.add)
                    dve.drain().then_inc(sem(f"t_ev0.{l}"), 1)

                def hidden(b, par):
                    dve.wait_ge(sem(f"a_mt.{l}"), count(f"a_mt.{l}", b + 1))
                    stt(mh1, mth, 1.0, bank[2 + par][:, 0:FH], ALU.add, ALU.mult)
                    dve.drain()
                    if due(b):
                        dve.wait_ge(sem(f"pe_ht.{l}"), count(f"pe_ht.{l}", b))
                    dve.tensor_tensor(hid, mh1, bank[2 + par][:, FH:2 * FH], ALU.mult).then_inc(sem(f"d_hid.{l}"), 1)

                def result(b, par, n):
                    dve.wait_ge(sem(f"pe_o.{l}"), count(f"pe_o.{l}", b + 1))
                    if due(n * 16):
                        dve.wait_ge(sem(f"y_stored_{par}.{l}"), count(f"y_stored_{par}.{l}", n * 16))
                    dve.tensor_tensor(yo[par][:, 0:512], bank[6][:], gatebc[:, 0:512], ALU.mult)
                    dve.tensor_tensor(yo[par][:, 512:], bank[7][:], gatebc[:, 512:], ALU.mult)
                    dve.drain().then_inc(sem(f"d_yo.{l}"), 1)

                turned(0, 0)
                hidden(0, 0)
                turned(1, 1)
                hidden(1, 1)
                turned(2, 0)
                result(0, 0, 0)

                def pair(i, turn_last):
                    for par in range(2):
                        b, n = i * 2 + par, i + par
                        hidden(b, par)
                        if par == 0 or turn_last:
                            turned(b + 1, 1 - par)
                        result(b - 1, 1 - par, n - 1)

                with dve.Fori(1, NE // 2 - 1) as ii:
                    pair(ii, True)
                pair(NE // 2 - 1, False)
                filling = overflow(dve, l)
                with dve.If(filling > 0):
                    turned(NE, 0)
                with dve.Fori(NE // 2, (NB + 1) // 2) as ii:
                    for par in range(2):
                        b, n = ii * 2 + par, ii + par
                        with filled(dve, 0, filling, b):
                            hidden(b, par)
                        with filled(dve, -1, filling, b):
                            turned(b + 1, 1 - par)
                        with filled(dve, 1, filling, b):
                            result(b - 1, 1 - par, n - 1)

                if l == 0:
                    gate(2, (2, 3), gatebc1)
                for tt in range(NT):
                    dve.wait_ge(sem(f"yg_{tt}.{l}"), count(f"yg_{tt}.{l}", 32))
                    stt(x[:, tt], yg[tt][0], wc1[:, tt:tt + 1], x[:, tt], ALU.mult, ALU.add)
                    dve.drain()
                    stt(x[:, tt], yg[tt][1], wc2[:, tt:tt + 1], x[:, tt], ALU.mult, ALU.add
                        ).then_inc(sem(f"x_up.{2 + 2 * l}"), 1)
                return filling

            filling = moe(0)

            norm(2)
            top_up(dve, filling, (("t_ev0", 1), ("d_hid", 1), ("d_yo", 1)))
            dve.wait_ge(sem("pe_wi"), 1)
            dve.tensor_scalar(wi.rearrange("p t h -> p (t h)"), bank[2][:, 0:NT * IH], IH ** -0.5, None, ALU.mult).then_inc(sem("d_wi"), 1)
            dve.tensor_copy(sel[:, 0, 0:P], causal[:])
            dve.drain()

            def index(tt):
                w = (tt + 1) * P
                s = sel[:, tt, 0:w]
                n = (tt - 1) * IH
                for h in range(IH):
                    dve.wait_ge(sem("a_rel"), n + h + 1)
                    if h == 0:
                        dve.tensor_scalar(s, rel[(n + h) % 2][:, 0:w], wi[:, tt, 0:1], None, ALU.mult).then_inc(sem("d_acc"), 1)
                    else:
                        stt(s, rel[(n + h) % 2][:, 0:w], wi[:, tt, h:h + 1], s, ALU.mult, ALU.add).then_inc(sem("d_acc"), 1)
                    dve.drain()

            def choose(tt):
                w = (tt + 1) * P
                s = sel[:, tt, 0:w]
                tt_(sel[:, tt, tt * P:w], sel[:, tt, tt * P:w], causal[:], ALU.add)
                for _ in range(TOPK // 8):
                    dve.max(out=max8, in_=s)
                    dve.drain()
                    dve.match_replace(out=s, in_to_replace=max8, in_values=s, imm_value=TAKEN)
                    dve.drain()
                dve.tensor_scalar(s, s, TAKEN * 0.5, NEG, ALU.is_gt, ALU.mult)
                dve.drain()

            index(1)
            choose(1)
            for tt in range(NT):
                b0 = 3 * (tt % 2)
                dve.wait_ge(sem("a_sqs"), tt + 1)
                dve.tensor_reduce(hss, sqs.rearrange("p (h d) -> p h d", d=HD), AX.X, ALU.add).then_inc(sem("d_hss"), 1)
                dve.wait_ge(sem("p_hrs"), tt + 1)
                if due(3 * tt):
                    dve.wait_ge(sem("pe_qk"), 3 * tt)
                for i in range(2):
                    dve.tensor_tensor(heads(qkn[:, i * 512:(i + 1) * 512]), heads(bank[b0 + i][:]),
                                      bc(hrs[:, 8 * i:8 * i + 8], HD), ALU.mult)
                for i in range(2):
                    dve.tensor_tensor(qkn[:, D:].rearrange("p (h r d) -> p r h d", r=2, d=HD)[:, i],
                                      heads(bank[b0 + 2][:, 0:KVH * HD]), bc(hrs[:, QH:], HD), ALU.mult)
                dve.drain().then_inc(sem("d_qkn"), 1)
                if tt < 2:
                    index(tt + 2)
                    choose(tt + 2)
            def mask_scores(u):
                tt, kv = u // 4, u % 4
                w = (tt + 1) * P
                for i in range(4):
                    dve.wait_ge(sem("pe_s"), 4 * u + i + 1)
                    if i == 0:
                        if due(chunks_before(u - 1)):
                            dve.wait_ge(sem("pe_pt"), chunks_before(u - 1))
                        if u > 3:
                            dve.wait_ge(sem("a_exp"), 4 * (u - 3))
                    dve.tensor_tensor_reduce(out=Sm[u % 2][:, i, 0:w], in0=bank[i][:, 0:w], in1=sel[:, tt, 0:w],
                                             scale=HD ** -0.5, scalar=-3e38, op0=ALU.add, op1=ALU.max,
                                             accum_out=nmx[:, kv, i:i + 1]).then_inc(sem("d_sm"), 1)
                dve.drain()
                dve.tensor_scalar(nmx[:, kv], nmx[:, kv], -1.0, None, ALU.mult).then_inc(sem("d_nmx"), 1)

            def turned_out(u):
                base = chunks_before(u)
                for c in range(u // 4 + 1):
                    if (base + c) % 2 == 1:
                        dve.wait_ge(sem("pe_pt"), base + c + 1)
                        if due(u):
                            dve.wait_ge(sem("pe_pv"), u)
                        dve.tensor_copy(PT[:, c, :], bank[5][:]).then_inc(sem("d_pt"), 1)

            def output(tt):
                dve.wait_ge(sem("a_exp"), 16 * (tt + 1))
                dve.reciprocal(rinv, rsum[:, tt % 2])
                dve.drain()
                dve.wait_ge(sem("pe_pv"), 4 * (tt + 1))
                for hh in range(2):
                    dve.tensor_tensor(heads(o[:, hh * 512:(hh + 1) * 512]), heads(bank[6 + hh][:]),
                                      bc(rinv[:, 8 * hh:8 * hh + 8], HD), ALU.mult)
                dve.drain().then_inc(sem("d_o"), 1)
                for hh in range(2):
                    half = slice(hh * 512, (hh + 1) * 512)
                    dve.wait_ge(sem("pe_xo"), 2 * tt + hh + 1)
                    dve.tensor_tensor(o[:, half], bank[6 + hh][:], gatebc1[:, half], ALU.mult).then_inc(sem("d_xo"), 1)
                dve.drain()
                dve.tensor_tensor(x[:, tt], x[:, tt], o, ALU.add).then_inc(sem("x_up.3"), 1)
                dve.drain()

            for u in range(17):
                if u < 16:
                    mask_scores(u)
                if u > 0:
                    turned_out(u - 1)
                    if u % 4 == 0:
                        output(u // 4 - 1)
            moe(1)


INPUTS = ["x", "c", "ada_w", "ada_b", "norm_mix", "norm_ffn", "ssd_w_in", "ssd_conv_w", "ssd_conv_b", "ssd_dt_bias",
          "ssd_a_log", "ssd_d", "ssd_norm", "ssd_w_out", "dsa_w_in", "dsa_q_norm", "dsa_k_norm", "dsa_w_out",
          "moe_w_group", "moe_b_group", "moe_w_expert", "moe_b_expert", "moe_w1", "moe_w3", "moe_w2"]


def kernel(**inputs):
    import concourse.bacc as bacc
    from concourse.bass_utils import run_bass_kernel_spmd

    nc = bacc.Bacc("TRN2", target_bir_lowering=False, num_devices=1)
    arrays, tensors = {}, {}
    for name in INPUTS:
        a = np.ascontiguousarray(inputs[name])
        arrays["in_" + name] = a
        tensors[name] = nc.dram_tensor("in_" + name, a.shape, mybir.dt.from_np(a.dtype), kind="ExternalInput").ap()
    tensors["out"] = nc.dram_tensor("out", (1, SEQ, D), F32, kind="ExternalOutput").ap()
    build(nc, tensors)
    result = run_bass_kernel_spmd(nc, [arrays], core_ids=[0])
    return result.results[0]["out"]
```
